# Optimizing a Trainium2 kernel written in Bass

```python
import math
import jax, jax.numpy as jnp
from jax import lax
import numpy as np

D_MODEL = 1024
BATCH = 1
SEQ = 256
DEPTH = 1

D_RNN = 1024
RNN_BLOCKS = 16
RNN_BLOCK = D_RNN // RNN_BLOCKS
CONV_W = 4
RGLRU_C = 8.0
N_HEADS = 8
HEAD_DIM = 64
V_DIM = 2 * HEAD_DIM
ATT_QK = N_HEADS * 2 * HEAD_DIM
ATT_V = N_HEADS * V_DIM
Q_BLOCK = 128
N_BRANCH = 2
D_IN = 2 * D_RNN + 2 * ATT_QK + ATT_V + N_BRANCH * D_MODEL
NUM_BUCKETS = 32
MAX_EXACT = NUM_BUCKETS // 2
MAX_DISTANCE = 128
N_EXPERTS = 32
TOP_K = 4
D_FF = D_MODEL
SWIGLU_LIMIT = 7.0
SWIGLU_ALPHA = 1.702
MOE_BLOCK = 128
EPS = 1e-6
NEG_INF = -1e30

kernel_name = 'hybrid_rglru_diffattn_moe_block'

def rms_norm(x, g):
    xf = x.astype(jnp.float32)
    y = xf * lax.rsqrt(jnp.mean(xf * xf, axis=-1, keepdims=True) + EPS)
    return (y * g.astype(jnp.float32)).astype(x.dtype)

def lambda_init(layer):
    return 0.8 - 0.6 * math.exp(-0.3 * layer)

def rel_bucket(q_pos, k_pos):
    n = jnp.maximum(q_pos[:, None] - k_pos[None, :], 0)
    nf = jnp.maximum(n, MAX_EXACT).astype(jnp.float32)
    large = MAX_EXACT + (jnp.log(nf / MAX_EXACT) / math.log(MAX_DISTANCE / MAX_EXACT) * (NUM_BUCKETS - MAX_EXACT)).astype(jnp.int32)
    large = jnp.minimum(large, NUM_BUCKETS - 1)
    return jnp.where(n < MAX_EXACT, n, large)

def _lru_combine(c1, c2):
    a1, b1 = c1
    a2, b2 = c2
    return a1 * a2, a2 * b1 + b2

def rglru_branch(xr, gate, conv_w, conv_b, w_a, b_a, w_x, b_x, lru_lambda):
    B, S, _ = xr.shape
    xc = lax.conv_general_dilated(xr, conv_w[:, None, :].astype(xr.dtype), window_strides=(1,), padding=[(CONV_W - 1, 0)], dimension_numbers=('NWC', 'WIO', 'NWC'), feature_group_count=D_RNN) + conv_b
    xb = xc.reshape(B, S, RNN_BLOCKS, RNN_BLOCK)
    r = jax.nn.sigmoid(jnp.einsum('bsnc,ncd->bsnd', xb, w_a) + b_a).reshape(B, S, D_RNN)
    i = jax.nn.sigmoid(jnp.einsum('bsnc,ncd->bsnd', xb, w_x) + b_x).reshape(B, S, D_RNN)
    log_a = -RGLRU_C * r.astype(jnp.float32) * jax.nn.softplus(-lru_lambda.astype(jnp.float32))
    a = jnp.exp(log_a)
    mult = jnp.sqrt(-jnp.expm1(2.0 * log_a))
    u = mult * (i * xc).astype(jnp.float32)
    _, h = lax.associative_scan(_lru_combine, (a, u), axis=1)
    return h.astype(xr.dtype) * jax.nn.gelu(gate, approximate=True)

def diff_attention(q, k, v, lam, lam_init, subln_g, rel_table):
    B, S = q.shape[0], q.shape[1]
    qt = q.transpose(3, 0, 2, 1, 4)
    kt = k.transpose(3, 0, 2, 1, 4)
    vt = v.transpose(0, 2, 1, 3)
    k_pos = jnp.arange(S, dtype=jnp.int32)
    scale = HEAD_DIM ** -0.5

    def block(blk):
        start = blk * Q_BLOCK
        qb = lax.dynamic_slice_in_dim(qt, start, Q_BLOCK, axis=3)
        q_pos = start + jnp.arange(Q_BLOCK, dtype=jnp.int32)
        bias = rel_table[rel_bucket(q_pos, k_pos)].transpose(2, 0, 1).astype(jnp.float32)
        mask = k_pos[None, :] <= q_pos[:, None]
        s = jnp.einsum('nbhqd,nbhkd->nbhqk', qb, kt).astype(jnp.float32) * scale + bias
        p = jax.nn.softmax(jnp.where(mask, s, NEG_INF), axis=-1)
        w = p[0] - lam * p[1]
        return jnp.einsum('bhqk,bhkd->bhqd', w.astype(v.dtype), vt)

    o = lax.map(block, jnp.arange(S // Q_BLOCK, dtype=jnp.int32))
    o = o.transpose(1, 0, 3, 2, 4).reshape(B, S, N_HEADS, V_DIM)
    o = rms_norm(o, subln_g) * (1.0 - lam_init)
    return o.reshape(B, S, ATT_V)

def moe_ffn(h, w_router, b_router, w_gate_e, b_gate_e, w_up_e, b_up_e, w_down_e, b_down_e):
    B, S, D = h.shape
    T = B * S
    TK = T * TOP_K
    xt = h.reshape(T, D)
    logits = (xt @ w_router + b_router).astype(jnp.float32)
    top_val, top_idx = lax.top_k(logits, TOP_K)
    weights = jax.nn.softmax(top_val, axis=-1)
    flat_e = top_idx.reshape(-1)
    flat_tok = jnp.arange(TK, dtype=jnp.int32) // TOP_K
    flat_w = weights.reshape(-1)
    order = jnp.argsort(flat_e)
    s_e, s_tok, s_w = flat_e[order], flat_tok[order], flat_w[order]
    counts = jnp.bincount(flat_e, length=N_EXPERTS)
    starts = jnp.cumsum(counts) - counts
    padded = (counts + MOE_BLOCK - 1) // MOE_BLOCK * MOE_BLOCK
    ends_p = jnp.cumsum(padded)
    starts_p = ends_p - padded
    dest = starts_p[s_e] + (jnp.arange(TK, dtype=jnp.int32) - starts[s_e])
    n_blocks = TK // MOE_BLOCK + N_EXPERTS
    P = n_blocks * MOE_BLOCK
    slot_tok = jnp.full((P,), T, dtype=jnp.int32).at[dest].set(s_tok)
    slot_w = jnp.zeros((P,), jnp.float32).at[dest].set(s_w)
    block_expert = jnp.minimum(jnp.searchsorted(ends_p, jnp.arange(n_blocks, dtype=jnp.int32) * MOE_BLOCK, side='right'), N_EXPERTS - 1)
    x_slots = xt.at[slot_tok].get(mode='fill', fill_value=0).reshape(n_blocks, MOE_BLOCK, D)

    def expert_block(args):
        xb, e = args
        g = xb @ w_gate_e[e] + b_gate_e[e]
        u = xb @ w_up_e[e] + b_up_e[e]
        g = jnp.minimum(g, SWIGLU_LIMIT)
        u = jnp.clip(u, -SWIGLU_LIMIT, SWIGLU_LIMIT)
        act = (u + 1.0) * (g * jax.nn.sigmoid(SWIGLU_ALPHA * g))
        return act @ w_down_e[e] + b_down_e[e]

    y_slots = lax.map(expert_block, (x_slots, block_expert)).reshape(P, D)
    y = jnp.zeros((T, D), h.dtype).at[slot_tok].add(slot_w[:, None].astype(h.dtype) * y_slots, mode='drop')
    return y.reshape(B, S, D)

def setup_inputs(seed: int = 0) -> dict:
    key = jax.random.key(seed)
    ks = jax.random.split(key, 32)
    L = DEPTH

    def nrm(k, shape, scale):
        return jax.random.normal(k, shape, jnp.float32) * scale

    a0 = jax.random.uniform(ks[9], (L, D_RNN), jnp.float32, 0.9, 0.999)
    return {
        'x': nrm(ks[0], (BATCH, SEQ, D_MODEL), 1.0),
        'norm_mix_g': 1.0 + nrm(ks[1], (L, D_MODEL), 0.05),
        'w_in': nrm(ks[2], (L, D_MODEL, D_IN), D_MODEL ** -0.5),
        'conv_w': nrm(ks[3], (L, CONV_W, D_RNN), CONV_W ** -0.5),
        'conv_b': nrm(ks[4], (L, D_RNN), 0.02),
        'w_rg_a': nrm(ks[5], (L, RNN_BLOCKS, RNN_BLOCK, RNN_BLOCK), RNN_BLOCK ** -0.5),
        'b_rg_a': nrm(ks[6], (L, RNN_BLOCKS, RNN_BLOCK), 0.02),
        'w_rg_x': nrm(ks[7], (L, RNN_BLOCKS, RNN_BLOCK, RNN_BLOCK), RNN_BLOCK ** -0.5),
        'b_rg_x': nrm(ks[8], (L, RNN_BLOCKS, RNN_BLOCK), 0.02),
        'lru_lambda': jnp.log(a0) - jnp.log1p(-a0),
        'diff_lambda_q1': nrm(ks[10], (L, HEAD_DIM), 0.1),
        'diff_lambda_k1': nrm(ks[11], (L, HEAD_DIM), 0.1),
        'diff_lambda_q2': nrm(ks[12], (L, HEAD_DIM), 0.1),
        'diff_lambda_k2': nrm(ks[13], (L, HEAD_DIM), 0.1),
        'subln_g': 1.0 + nrm(ks[14], (L, V_DIM), 0.05),
        'rel_bias_table': nrm(ks[15], (NUM_BUCKETS, N_HEADS), 0.3),
        'w_proj_rnn': nrm(ks[16], (L, D_RNN, D_MODEL), D_RNN ** -0.5),
        'w_proj_att': nrm(ks[17], (L, ATT_V, D_MODEL), ATT_V ** -0.5),
        'w_out': nrm(ks[18], (L, D_MODEL, D_MODEL), D_MODEL ** -0.5),
        'norm_ffn_g': 1.0 + nrm(ks[19], (L, D_MODEL), 0.05),
        'w_router': nrm(ks[20], (L, D_MODEL, N_EXPERTS), D_MODEL ** -0.5),
        'b_router': nrm(ks[21], (L, N_EXPERTS), 0.01),
        'w_gate_e': nrm(ks[22], (L, N_EXPERTS, D_MODEL, D_FF), D_MODEL ** -0.5),
        'b_gate_e': nrm(ks[23], (L, N_EXPERTS, D_FF), 0.02),
        'w_up_e': nrm(ks[24], (L, N_EXPERTS, D_MODEL, D_FF), D_MODEL ** -0.5),
        'b_up_e': nrm(ks[25], (L, N_EXPERTS, D_FF), 0.02),
        'w_down_e': nrm(ks[26], (L, N_EXPERTS, D_FF, D_MODEL), D_FF ** -0.5),
        'b_down_e': nrm(ks[27], (L, N_EXPERTS, D_MODEL), 0.02),
        'norm_final_g': 1.0 + nrm(ks[28], (D_MODEL,), 0.05),
    }

def reference(x, norm_mix_g, w_in, conv_w, conv_b, w_rg_a, b_rg_a, w_rg_x, b_rg_x, lru_lambda, diff_lambda_q1, diff_lambda_k1, diff_lambda_q2, diff_lambda_k2, subln_g, rel_bias_table, w_proj_rnn, w_proj_att, w_out, norm_ffn_g, w_router, b_router, w_gate_e, b_gate_e, w_up_e, b_up_e, w_down_e, b_down_e, norm_final_g):
    B, S, D = x.shape
    o0 = 0
    o1 = o0 + D_RNN
    o2 = o1 + D_RNN
    o3 = o2 + ATT_QK
    o4 = o3 + ATT_QK
    o5 = o4 + ATT_V
    for l in range(DEPTH):
        h = rms_norm(x, norm_mix_g[l])
        proj = h @ w_in[l]
        xr, gr = proj[..., o0:o1], proj[..., o1:o2]
        q = proj[..., o2:o3].reshape(B, S, N_HEADS, 2, HEAD_DIM)
        k = proj[..., o3:o4].reshape(B, S, N_HEADS, 2, HEAD_DIM)
        v = proj[..., o4:o5].reshape(B, S, N_HEADS, V_DIM)
        gates = jax.nn.sigmoid(proj[..., o5:].reshape(B, S, N_BRANCH, D_MODEL))

        y_rnn = rglru_branch(xr, gr, conv_w[l], conv_b[l], w_rg_a[l], b_rg_a[l], w_rg_x[l], b_rg_x[l], lru_lambda[l])
        lam_init = lambda_init(l)
        lam = (jnp.exp(jnp.sum(diff_lambda_q1[l].astype(jnp.float32) * diff_lambda_k1[l].astype(jnp.float32)))
               - jnp.exp(jnp.sum(diff_lambda_q2[l].astype(jnp.float32) * diff_lambda_k2[l].astype(jnp.float32))) + lam_init)
        y_att = diff_attention(q, k, v, lam, lam_init, subln_g[l], rel_bias_table)

        merged = gates[..., 0, :] * (y_rnn @ w_proj_rnn[l]) + gates[..., 1, :] * (y_att @ w_proj_att[l])
        x = x + merged @ w_out[l]
        hf = rms_norm(x, norm_ffn_g[l])
        x = x + moe_ffn(hf, w_router[l], b_router[l], w_gate_e[l], b_gate_e[l], w_up_e[l], b_up_e[l], w_down_e[l], b_down_e[l])
    return rms_norm(x, norm_final_g)


_drawn_inputs = setup_inputs


def setup_inputs(seed=0):
    import zlib

    import numpy as np

    out = dict(_drawn_inputs(seed))
    spreads = {}
    factors = {'b_rg_a': 20.541,
     'b_rg_x': 14.037,
     'diff_lambda_q1': 4.374,
     'b_gate_e': 6.717,
     'b_up_e': 8.0,
     'b_down_e': 6.354,
     'b_router': 2.73}
    for name, (base, spread) in spreads.items():
        noise = np.random.default_rng([zlib.crc32(name.encode()), seed]).standard_normal(out[name].shape)
        drawn = base * np.exp(spread * noise) if base else spread * noise
        out[name] = __import__('jax').numpy.asarray(drawn.astype(out[name].dtype))
    for name, factor in factors.items():
        out[name] = (out[name] * factor).astype(out[name].dtype)
    return out
```

```python
import math
from contextlib import ExitStack

import numpy as np

import concourse.bass as bass
from concourse import mybir

F32 = mybir.dt.float32
I32 = mybir.dt.int32
ALU = mybir.AluOpType
ACT = mybir.ActivationFunctionType
AX_X = mybir.AxisListType.X

P = 128
D = 1024
KC = D // P
T = 256
TT = T // P
H = 8
HD = 64
VD = 128
RB = 64
NBUCKET = 32
NE = 32
TOPK = 4
JB = 64
JOBS = 48
CH = 512
NQ = 4
DIFFS = 384
EPS = 1e-6
NEG = -1e30
LIMIT = 7.0
SWIGLU_ALPHA = 1.702
RGLRU_C = 8.0
LAM_INIT = 0.8 - 0.6 * math.exp(-0.3 * 0)
GELU_A = 0.044715
GELU_B = math.sqrt(2.0 / math.pi)

V_NORM, V_CONVW, V_CONVB, V_BA, V_BX, V_LAM, V_SUB = 0, 8, 40, 48, 56, 64, 72
NV = 73

MIX = ["xr", "v", "q", "k", "gr", "g0", "g1"]
COLUMN = {"xr": 0, "gr": D, "q": 2 * D, "k": 3 * D, "v": 4 * D, "g0": 5 * D, "g1": 6 * D}
STREAM = [(m, c) for m in MIX + ["prnn", "patt", "out"] for c in range(D // CH)]
UNITS = [(m, c, b) for m, c in STREAM for b in range(2)]


def unit(name, n=0):
    return [i for i, (m, _, _) in enumerate(UNITS) if m == name][n]


def bucket_onehot():
    out = np.zeros((NBUCKET + 1, DIFFS), np.float32)
    half = NBUCKET // 2
    for m in range(DIFFS):
        n = T - 1 - m
        if n < 0:
            b = NBUCKET
        elif n < half:
            b = n
        else:
            b = min(half + int(math.log(n / half) / math.log(128 / half) * half), NBUCKET - 1)
        out[b, m] = 1.0
    return out


SIGNALS = """x_loaded vectors_loaded block_diagonals_cleared block_diagonals_loaded onehot_loaded
rel_loaded lambda_vectors_loaded bias_vector_stored bias_tile_loaded router_loaded norm_rows_loaded
bias_rows_loaded x_again_loaded out_stored
identity_ready constants_ready query_zeros_ready bias_rows_cleared job_tiles_cleared
x_squared x_std x_normed vectors_turned vectors_ready norm_turned norm_ready bias_vector_done
bias_vector_ready lambda_sums_ready lambda_exps_ready lambda_ready softplus_in softplus_exp
softplus_ready conv_ready gates_done gates_out gates_ready decay_ready multiplier_in
multiplier_ready scan_ready gelu_square gelu_in gelu_tanh rnn_ready
scores_done scores_ready exps_done weights_ready weights_turned weights_out head_done head_out
heads_squared heads_summed heads_ms heads_std att_ready merged mixed
unit_done unit_out projection_out chunk_used
mixed_half_squared mixed_squared mixed_ms mixed_std ffn_ready ffn_turned ffn_turned_out
logits_turned logits_biased logits_done logits_ready top_ready route_exps route_ready route_turned
route_out overflow_ready ends_done jobs_ready job_columns_done job_columns_ready job_table_ready
sums_opened result_ready result_half_squared result_squared result_ms result_std fin""".split()

JOB_SIGNALS = """selection gathered gather_out gather_turned input expert_onehot gate_done gate_clamped
sigmoid up_done up_clamped product activation weighted_selection scatter_turned scatter_ready
activation_turned activation_out down_done output_out scattered""".split()


def hybrid_block(nc, A, out):
    with ExitStack() as ctx:
        def sb(name, shape, dt=F32):
            return ctx.enter_context(nc.sbuf_tensor(name, shape, dt))

        def sem(name):
            return ctx.enter_context(nc.semaphore(name))

        WG = sb("w_gate_sb", [P, KC, D])
        WU = sb("w_up_sb", [P, KC, D])
        WD = sb("w_down_sb", [P, KC, D])
        wst = WD[:, :, :].rearrange("p a n -> p (a n)").rearrange("p (s k n) -> p s k n", s=2, k=KC)
        arena = sb("arena", [P, 12, 2048])

        def tile(n, a=KC, off=0, size=2048):
            return arena[:, n, off:off + size].rearrange("p (a b) -> p a b", a=a)

        hT = tile(0)
        hn = tile(1, TT)
        oT = tile(1)
        xrT = tile(2)
        xcT = tile(3)
        rT = tile(4)
        iT = tile(5)
        yrT = tile(6)
        onehot = arena[0:NBUCKET + 1, 6, 0:DIFFS]
        bias_vec = arena[0:H, 6, DIFFS:2 * DIFFS]
        blkd = tile(7, 16)
        qz = [tile(7), tile(8)]
        osq = tile(7)
        orr = tile(8)
        kT = tile(9)
        yaT = tile(9)
        vS = tile(10, TT)
        x2 = tile(10, TT)
        tb = tile(11)
        g2row, gfrow = arena[:, 0, 0:D], arena[:, 0, D:2 * D]
        xg, xgT = arena[:, 2, 0:512], tile(2, 4, 512, 512)
        gm, uc = arena[:, 2, 1024:1536], arena[:, 2, 1536:2048]
        sg, av = arena[:, 3, 0:512], arena[:, 3, 512:1024]
        avT, ys = tile(3, 4, 1024, 512), arena[:, 3, 1536:2048]
        swz = arena[:, 4, 0:512].rearrange("p (h t n) -> p h t n", h=2, t=TT)
        sel = tile(4, TT, 512, TT * JB)
        selw = tile(4, TT, 640, TT * 2 * JB)
        ohb = arena[:, 4, 896:896 + JB]
        jcol = tile(4, TT, 1024, TT * JOBS)
        gcol = tile(4, TT, 1024 + TT * JOBS, TT * JOBS)
        ohj = arena[:, 4, 1280:1280 + JOBS]
        brow = arena[:, 6, :].rearrange("p (m n) -> p m n", m=2)
        h2 = tile(7, TT)
        hfT = tile(8)
        junk = arena[:, 9, 0:D]
        bdrow = arena[0:NE, 9, D:2 * D]

        def rt(off, *shape):
            ap = arena[:, 11, off:off + math.prod(shape)]
            return ap.rearrange("p (a b) -> p a b", a=shape[0]) if len(shape) == 2 else ap
        r_log, r_gt, r_eq, r_rank, r_exp = (rt(64 * n, TT, NE) for n in range(5))
        r_mask, r_gate = rt(320, TT, NE), rt(384, TT, NE)
        r_max, r_nmx, r_ngt, r_need = rt(448, TT, 8), rt(464, TT), rt(466, TT), rt(468, TT)
        r_sum, r_inv = rt(470, TT), rt(472, TT)
        r_logT = arena[0:NE, 11, 512:512 + T]
        r_tabT = arena[0:NE, 11, 768:768 + 2 * T]
        maskT, gateT = arena[0:NE, 11, 768:768 + T], arena[0:NE, 11, 768 + T:768 + 2 * T]
        inclT, slotT = arena[0:NE, 11, 1280:1280 + T], arena[0:NE, 11, 1536:1536 + T]
        novf, ends, starts = (arena[0:NE, 11, 1792 + n:1793 + n] for n in range(3))
        block64, owork = arena[0:NE, 11, 1800:1800 + JOBS], arena[0:NE, 11, 1850:1850 + JOBS - NE]

        ident = sb("ident", [P, P])
        ones = sb("ones", [P, T])
        iota_slot = sb("iota_slot", [P, 2 * JB])
        iota_job = sb("iota_job", [NE, JOBS])
        tri = sb("tri", [NE, NE])
        ecol = sb("ecol", [NE, 1])
        pv = sb("pv", [NV, P])
        pvT = sb("pvT", [P, NV])
        sp = sb("sp", [P, 8, KC])
        wr = sb("wr", [P, KC, NE])
        brt = sb("brt", [NE, 1])
        rel = sb("rel", [NBUCKET + 1, H])
        lamv = sb("lamv", [P, 4, HD])
        lam = sb("lam", [P, 8])
        small = sb("small", [P, 12])
        sc = sb("sc", [P, 2, 768])
        wm = sb("wm", [P, 384])
        wT = sb("wT", [P, 384])
        st = sb("st", [P, 2, 12])
        jobi = sb("jobi", [1, 64], I32)

        bank = [ctx.enter_context(nc.psum_tensor(f"bank{i}", [P, 512], F32)) for i in range(8)]

        def halves(ps):
            return ps[:, :].rearrange("p (a b) -> p a b", a=2)

        def quarters(ps):
            return ps[:, :].rearrange("p (a b) -> p a b", a=4)

        head_size = P * (DIFFS + 1)
        scratch = nc.dram_tensor("bias_scratch", (H, head_size), F32, kind="Internal").ap()

        s = {n: sem(n) for n in SIGNALS}
        job = {n: sem(f"job_{n}") for n in JOB_SIGNALS}
        chunk_loaded = [sem("chunk_loaded_0"), sem("chunk_loaded_1")]
        loaded = {m: [sem(f"{m}_loaded_{q}") for q in range(NQ)] for m in ("gate", "up", "down")}
        used = {m: sem(f"{m}_used") for m in ("gate", "up", "down")}
        dve_order = sem("dve_order")
        W_EXP = {"gate": (A["w_gate_e"], WG), "up": (A["w_up_e"], WU), "down": (A["w_down_e"], WD)}

        def broadcast(a, shape):
            return bass.AP(a.tensor, a.offset, [[0, P], [1, shape]])

        block = ctx.enter_context(nc.Block())

        @block.sync
        def _(eng):
            for t in range(TT):
                eng.dma_start(hn[:, t, :], A["x"][0, t * P:(t + 1) * P, :]).then_inc(s["x_loaded"], 16)
            for r, a in ((V_NORM, A["norm_mix_g"]), (V_CONVB, A["conv_b"]), (V_LAM, A["lru_lambda"])):
                eng.dma_start(pv[r:r + KC, :], a.rearrange("l (c p) -> (l c) p", p=P)).then_inc(s["vectors_loaded"], 16)
            eng.dma_start(pv[V_CONVW:V_CONVW + 4 * KC, :], A["conv_w"].rearrange("l w (c p) -> (l w c) p", p=P)
                          ).then_inc(s["vectors_loaded"], 16)
            for r, a in ((V_BA, A["b_rg_a"]), (V_BX, A["b_rg_x"])):
                eng.dma_start(pv[r:r + KC, :], a.rearrange("l (c b) d -> (l c) (b d)", b=2)
                              ).then_inc(s["vectors_loaded"], 16)
            eng.dma_start(pv[V_SUB:V_SUB + 1, :], A["subln_g"]).then_inc(s["vectors_loaded"], 16)

            def chunk(i):
                m, c = STREAM[i]
                if m in COLUMN:
                    w, col = A["w_in"][0], COLUMN[m] + c * CH
                else:
                    w, col = A[{"prnn": "w_proj_rnn", "patt": "w_proj_att", "out": "w_out"}[m]][0], c * CH
                if i >= 2:
                    eng.wait_ge(s["chunk_used"], i - 1)
                eng.dma_start(wst[:, i % 2], w[:, col:col + CH].rearrange("(k p) n -> p k n", p=P)
                              ).then_inc(chunk_loaded[i % 2], 16)

            chunk(0)
            eng.dma_start(rel[0:NBUCKET, :], A["rel_bias_table"]).then_inc(s["rel_loaded"], 16)
            eng.dma_start(onehot, A["bucket_onehot"]).then_inc(s["onehot_loaded"], 16)
            chunk(1)
            for n, name in enumerate(["diff_lambda_q1", "diff_lambda_k1", "diff_lambda_q2", "diff_lambda_k2"]):
                eng.dma_start(lamv[:, n, :], broadcast(A[name], HD)).then_inc(s["lambda_vectors_loaded"], 16)
            eng.wait_ge(s["block_diagonals_cleared"], 1)
            for g, name in enumerate(["w_rg_a", "w_rg_x"]):
                for half in range(2):
                    src = A[name][0].rearrange("(n b) c d -> b c n d", b=2)[half]
                    eng.dma_start(blkd[half * RB:(half + 1) * RB, g * KC:(g + 1) * KC, half * RB:(half + 1) * RB],
                                  src).then_inc(s["block_diagonals_loaded"], 16)
            eng.dma_start(wr[:, :, :], A["w_router"][0].rearrange("(k p) e -> p k e", p=P)
                          ).then_inc(s["router_loaded"], 16)
            eng.dma_start(brt[:, :], A["b_router"].rearrange("l e -> e l")).then_inc(s["router_loaded"], 16)
            eng.wait_ge(s["bias_vector_ready"], 1)
            eng.dma_start(scratch.rearrange("h (q m) -> h q m", q=P)[:, :, 0:DIFFS],
                          bias_vec.rearrange("h (a m) -> h a m", a=1).to_broadcast([H, P, DIFFS])
                          ).then_inc(s["bias_vector_stored"], 16)
            chunk(2)
            eng.wait_ge(s["bias_vector_stored"], 16)
            back = bass.AP(scratch.tensor, scratch.offset + P - 1, [[DIFFS, P], [head_size, H], [1, T]])
            eng.dma_start(tb[:, :, :], back).then_inc(s["bias_tile_loaded"], 16)

            def expert_load(m, q, expert):
                w, place = W_EXP[m]
                rows = D // NQ
                src = w[0][expert, q * rows:(q + 1) * rows, :].rearrange("a (k p) n -> p (a k) n", p=P)
                eng.dma_start(place[:, q * KC // NQ:(q + 1) * KC // NQ, :], src).then_inc(loaded[m][q], 16)

            first_late = STREAM.index(("gr", 0))
            for i in range(3, len(STREAM)):
                chunk(i)
                if first_late <= i < first_late + NQ:
                    expert_load("gate", i - first_late, slice(0, 1))
                    expert_load("up", i - first_late, slice(0, 1))
                if i == STREAM.index(("prnn", 1)):
                    eng.dma_start(g2row, broadcast(A["norm_ffn_g"], D)).then_inc(s["norm_rows_loaded"], 16)
                    eng.dma_start(gfrow, broadcast(A["norm_final_g"], D)).then_inc(s["norm_rows_loaded"], 16)
                    eng.wait_ge(s["head_done"], H)
                    for t in range(TT):
                        eng.dma_start(x2[:, t, :], A["x"][0, t * P:(t + 1) * P, :]).then_inc(s["x_again_loaded"], 16)
            eng.wait_ge(s["bias_rows_cleared"], 1)
            eng.dma_start(brow[0:NE, 0, :], A["b_gate_e"][0]).then_inc(s["bias_rows_loaded"], 16)
            eng.dma_start(brow[0:NE, 1, :], A["b_up_e"][0]).then_inc(s["bias_rows_loaded"], 16)
            eng.wait_ge(s["unit_done"], unit("patt", 3) + 1)
            eng.dma_start(bdrow, A["b_down_e"][0]).then_inc(s["bias_rows_loaded"], 16)
            eng.wait_ge(s["chunk_used"], len(STREAM))
            for q in range(NQ):
                expert_load("down", q, slice(0, 1))
            eng.wait_ge(s["job_table_ready"], 1)
            jobs = eng.value_load(jobi[0:1, JOBS:JOBS + 1], min_val=NE, max_val=JOBS - 1)
            with eng.Fori(1, jobs) as j:
                expert = eng.value_load(jobi[0:1, bass.ds(j, 1)], min_val=0, max_val=NE - 1)
                for m in ("gate", "up", "down"):
                    for q in range(NQ):
                        eng.wait_ge(used[m], j * NQ + (q + 1 - NQ))
                        expert_load(m, q, bass.ds(expert, 1))
            for t in range(TT):
                eng.wait_ge(s["fin"], t + 1)
                eng.dma_start(out[0, t * P:(t + 1) * P, :], h2[:, t, :]).then_inc(s["out_stored"], 16)
            eng.wait_ge(s["out_stored"], 16 * TT)

        @block.gpsimd
        def _(eng):
            eng.memset(ident[:, :], 0.0).then_inc(s["identity_ready"], 1)
            eng.wait_ge(s["identity_ready"], 1)
            eng.affine_select(out=ident[:, :], in_=ident[:, :], compare_op=ALU.not_equal, fill=1.0, base=0,
                              pattern=[[-1, P]], channel_multiplier=1).then_inc(s["identity_ready"], 1)
            eng.wait_ge(s["identity_ready"], 2)
            eng.memset(rel[NBUCKET:NBUCKET + 1, :], NEG).then_inc(s["constants_ready"], 1)
            eng.wait_ge(s["constants_ready"], 1)
            eng.memset(blkd[:, :, :], 0.0).then_inc(s["block_diagonals_cleared"], 1)
            eng.wait_ge(s["block_diagonals_cleared"], 1)
            eng.memset(ones[:, :], 1.0).then_inc(s["constants_ready"], 1)
            eng.wait_ge(s["constants_ready"], 2)
            eng.iota(iota_slot[:, :].rearrange("p (a b) -> p a b", a=2), [[0, 2], [1, JB]], base=0,
                     channel_multiplier=0, allow_small_or_imprecise_dtypes=True).then_inc(s["constants_ready"], 1)
            eng.wait_ge(s["constants_ready"], 3)
            eng.iota(iota_job[:, :], [[1, JOBS]], base=0, channel_multiplier=0,
                     allow_small_or_imprecise_dtypes=True).then_inc(s["constants_ready"], 1)
            eng.wait_ge(s["constants_ready"], 4)
            eng.iota(ecol[:, :], [[1, 1]], base=0, channel_multiplier=1,
                     allow_small_or_imprecise_dtypes=True).then_inc(s["constants_ready"], 1)
            eng.wait_ge(s["constants_ready"], 5)
            eng.memset(tri[:, :], 1.0).then_inc(s["constants_ready"], 1)
            eng.wait_ge(s["constants_ready"], 6)
            eng.affine_select(out=tri[:, :], in_=tri[:, :], compare_op=ALU.is_ge, fill=0.0, base=0,
                              pattern=[[1, NE]], channel_multiplier=-1).then_inc(s["constants_ready"], 1)
            eng.wait_ge(s["constants_ready"], 7)
            eng.wait_ge(s["gates_done"], KC)
            eng.memset(qz[0][HD:P, :, :], 0.0).then_inc(s["query_zeros_ready"], 1)
            eng.wait_ge(s["query_zeros_ready"], 1)
            eng.memset(qz[1][0:HD, :, :], 0.0).then_inc(s["query_zeros_ready"], 1)
            eng.wait_ge(s["unit_done"], unit("prnn", 3) + 1)
            eng.memset(brow[:, :, :], 0.0).then_inc(s["bias_rows_cleared"], 1)
            eng.wait_ge(s["merged"], 4)
            eng.memset(swz[:, :, :, :], 0.0).then_inc(s["job_tiles_cleared"], 1)
            eng.wait_ge(s["job_tiles_cleared"], 1)
            eng.memset(ohj, 0.0).then_inc(s["job_tiles_cleared"], 1)

        @block.scalar
        def _(eng):
            eng.wait_ge(s["x_loaded"], 16 * TT)
            for t in range(TT):
                eng.activation(tile(2 + t)[:, 0:4, :].rearrange("p a b -> p (a b)"), hn[:, t, :], ACT.Square,
                               accum_out=small[:, t:t + 1]).then_inc(s["x_squared"], 1)
            eng.wait_ge(s["x_std"], 1)
            eng.activation(small[:, 4:6], small[:, 2:4], ACT.Sqrt).then_inc(s["x_std"], 1)
            eng.wait_ge(s["vectors_ready"], 1)
            for n in range(4):
                eng.wait_ge(s["norm_turned"], n + 1)
                for c in (2 * n, 2 * n + 1):
                    eng.activation(hT[:, c, :], bank[2 + n][:, (c % 2) * T:(c % 2 + 1) * T], ACT.Copy,
                                   scale=pvT[:, V_NORM + c:V_NORM + c + 1]).then_inc(s["norm_ready"], 1)
            eng.wait_ge(s["softplus_in"], 1)
            eng.activation(sp[:, 1, :], sp[:, 0, :], ACT.Exp, scale=-1.0).then_inc(s["softplus_exp"], 1)
            eng.wait_ge(s["lambda_sums_ready"], 2)
            eng.activation(lam[:, 2:4], lam[:, 0:2], ACT.Exp).then_inc(s["lambda_exps_ready"], 1)

            def unit_out(u):
                m, c, b = UNITS[u]
                ps = bank[u % 2]
                f = 4 * c + 2 * b
                eng.wait_ge(s["unit_done"], u + 1)
                if m == "v":
                    ins = eng.activation(vS[:, b, c * CH:(c + 1) * CH], ps[:, :], ACT.Copy)
                elif m == "q":
                    eng.wait_ge(s["query_zeros_ready"], 2)
                    eng.activation(qz[0][0:HD, f:f + 2, :], halves(ps)[0:HD], ACT.Copy, scale=HD ** -0.5)
                    ins = eng.activation(qz[1][HD:P, f:f + 2, :], halves(ps)[HD:P], ACT.Copy, scale=HD ** -0.5)
                elif m in ("g0", "g1"):
                    ins = eng.activation((iT if m == "g0" else rT)[:, f:f + 2, :], halves(ps), ACT.Tanh, scale=0.5)
                else:
                    if m == "gr":
                        eng.wait_ge(s["scan_ready"], 1)
                    ins = eng.activation({"xr": xrT, "k": kT, "gr": xrT}[m][:, f:f + 2, :], halves(ps), ACT.Copy)
                ins.then_inc(s["unit_out"], 1)

            for u in range(unit("xr"), unit("v", 3) + 1):
                unit_out(u)
            for n in range(KC):
                eng.wait_ge(s["gates_done"], n + 1)
                for b in range(2):
                    g, c = n // 4, 2 * (n % 4) + b
                    col = (V_BA, V_BX)[g] + c
                    ins = eng.activation((rT, iT)[g][:, c, :], bank[2 + n % 6][:, b * T:(b + 1) * T], ACT.Sigmoid,
                                         bias=pvT[:, col:col + 1])
                ins.then_inc(s["gates_out"], 1)
            for u in range(unit("q"), unit("q", 3) + 1):
                unit_out(u)
            eng.wait_ge(s["softplus_ready"], 1)
            eng.wait_ge(s["conv_ready"], 4)
            eng.wait_ge(s["gates_out"], KC)
            for c in range(KC):
                eng.activation(xrT[:, c, :], rT[:, c, :], ACT.Exp, scale=sp[:, 4, c:c + 1]
                               ).then_inc(s["decay_ready"], 1)
            unit_out(unit("k"))
            eng.wait_ge(s["bias_tile_loaded"], 16)
            for c in range(KC):
                eng.activation(yrT[:, c, :], rT[:, c, :], ACT.Tanh, scale=sp[:, 5, c:c + 1]
                               ).then_inc(s["decay_ready"], 1)
            unit_out(unit("k", 1))
            eng.wait_ge(s["multiplier_in"], 1)
            eng.activation(rT[:, :, :], rT[:, :, :], ACT.Sqrt).then_inc(s["multiplier_ready"], 1)
            unit_out(unit("k", 2))
            unit_out(unit("k", 3))

            def exps(h):
                b = h % 2
                eng.wait_ge(s["scores_ready"], h + 1)
                for n, (o, w) in enumerate(((0, 256), (256, 256), (512, 128), (640, 128))):
                    eng.activation(sc[:, b, o:o + w], sc[:, b, o:o + w], ACT.Exp, bias=st[:, b, n:n + 1],
                                   accum_out=st[:, b, 4 + n:5 + n]).then_inc(s["exps_done"], 1)

            def weights_out(h):
                if h >= 1:
                    eng.wait_ge(s["head_done"], h)
                eng.wait_ge(s["weights_turned"], h + 1)
                eng.activation(wT[:, :], bank[5][:, 0:384], ACT.Copy).then_inc(s["weights_out"], 1)

            def head_out(h):
                eng.wait_ge(s["head_done"], h + 1)
                eng.activation(oT[:, h, :], bank[6][:, 0:T], ACT.Copy
                               ).then_inc(s["head_out"], 1)

            for step in range(12):
                unit_out(unit("gr") + step)
                if step < H:
                    exps(step)
                if 1 <= step <= H:
                    weights_out(step - 1)
                if 2 <= step <= H + 1:
                    head_out(step - 2)
                if step == 4:
                    eng.wait_ge(s["unit_out"], unit("gr", 3) + 1)
                    eng.activation(xcT[:, :, :], xrT[:, :, :], ACT.Square).then_inc(s["gelu_square"], 1)
                if step == 7:
                    eng.wait_ge(s["gelu_in"], 1)
                    eng.activation(xcT[:, :, :], xcT[:, :, :], ACT.Tanh, scale=GELU_B).then_inc(s["gelu_tanh"], 1)
            eng.wait_ge(s["head_out"], H)
            eng.activation(osq[:, :, :], oT[:, :, :], ACT.Square).then_inc(s["heads_squared"], 1)
            eng.wait_ge(s["heads_ms"], 4)
            eng.activation(orr[:, :, :], orr[:, :, :], ACT.Sqrt).then_inc(s["heads_std"], 1)

            def squares(half, whole):
                eng.activation(junk, x2[:, 0, :], ACT.Square, accum_out=small[:, 0:1]).then_inc(half, 1)
                eng.wait_ge(half, 1)
                eng.activation(junk, x2[:, 1, :], ACT.Square, accum_out=small[:, 1:2]).then_inc(whole, 1)

            eng.wait_ge(s["mixed"], 4)
            squares(s["mixed_half_squared"], s["mixed_squared"])
            eng.wait_ge(s["mixed_ms"], 1)
            eng.activation(small[:, 4:6], small[:, 2:4], ACT.Sqrt).then_inc(s["mixed_std"], 1)
            for n in range(4):
                eng.wait_ge(s["ffn_turned"], n + 1)
                eng.activation(hfT[:, 2 * n:2 * n + 2, :], halves(bank[n]), ACT.Copy).then_inc(s["ffn_turned_out"], 1)
            eng.wait_ge(s["top_ready"], 1)
            for t in range(TT):
                eng.activation(r_exp[:, t, :], r_log[:, t, :], ACT.Exp, bias=r_nmx[:, t:t + 1]
                               ).then_inc(s["route_exps"], 1)
            eng.wait_ge(s["route_turned"], 1)
            eng.activation(r_tabT, bank[2][0:NE, :], ACT.Copy).then_inc(s["route_out"], 1)

            eng.sem_inc(job["activation_out"], 1)
            eng.sem_inc(job["output_out"], 1)
            eng.wait_ge(job["gathered"], 1)
            eng.activation(xg, bank[2][:, :], ACT.Copy).then_inc(job["gather_out"], 1)
            eng.wait_ge(job["gather_turned"], 1)
            eng.activation(xgT, quarters(bank[2]), ACT.Copy).then_inc(job["input"], 1)
            eng.wait_ge(s["job_table_ready"], 1)
            jobs = eng.value_load(jobi[0:1, JOBS:JOBS + 1], min_val=NE, max_val=JOBS - 1)
            with eng.Fori(0, jobs) as j:
                eng.wait_ge(job["activation"], j + 1)
                eng.wait_ge(job["gate_clamped"], j + 1)
                eng.activation(sg, gm, ACT.Sigmoid, scale=SWIGLU_ALPHA).then_inc(job["sigmoid"], 1)
                eng.wait_ge(job["gathered"], j + 2)
                eng.activation(xg, bank[2][:, :], ACT.Copy).then_inc(job["gather_out"], 1)
                eng.wait_ge(job["scattered"], j + 1)
                eng.wait_ge(job["scatter_turned"], j + 2)
                turned = bank[3][:, 0:TT * P].rearrange("p (t n) -> p t n", t=TT)
                eng.activation(swz[0:JB, 0], turned[0:JB], ACT.Copy)
                eng.activation(swz[JB:P, 1], turned[JB:P], ACT.Copy).then_inc(job["scatter_ready"], 1)
                eng.wait_ge(job["up_done"], j + 1)
                eng.wait_ge(job["gather_turned"], j + 2)
                eng.activation(xgT, quarters(bank[2]), ACT.Copy).then_inc(job["input"], 1)
                eng.wait_ge(job["activation_turned"], j + 2)
                eng.activation(avT, quarters(bank[0]), ACT.Copy).then_inc(job["activation_out"], 1)
                eng.wait_ge(job["down_done"], j + 1)
                eng.activation(ys, bank[3][:, :], ACT.Copy).then_inc(job["output_out"], 1)
            eng.wait_ge(s["result_ready"], 4)
            squares(s["result_half_squared"], s["result_squared"])
            eng.wait_ge(s["result_ms"], 1)
            eng.activation(small[:, 4:6], small[:, 2:4], ACT.Sqrt).then_inc(s["result_std"], 1)

        @block.vector
        def _(eng):
            count = [0]

            def link(ins):
                count[0] += 1
                ins.then_inc(dve_order, 1)
                eng.wait_ge(dve_order, count[0])

            eng.wait_ge(s["x_squared"], TT)
            eng.tensor_scalar(small[:, 2:4], small[:, 0:2], 1.0 / D, EPS, ALU.mult, ALU.add).then_inc(s["x_std"], 1)
            eng.wait_ge(s["x_std"], 2)
            link(eng.reciprocal(small[:, 6:8], small[:, 4:6]))
            for t in range(TT):
                eng.tensor_scalar(hn[:, t, :], hn[:, t, :], small[:, 6 + t:7 + t], None, ALU.mult
                                  ).then_inc(s["x_normed"], 1)
            eng.wait_ge(s["vectors_turned"], 1)
            eng.tensor_copy(pvT[:, :], bank[7][:, 0:NV]).then_inc(s["vectors_ready"], 1)
            eng.wait_ge(s["bias_vector_done"], 1)
            eng.tensor_copy(bias_vec, bank[6][0:H, 0:DIFFS]).then_inc(s["bias_vector_ready"], 1)
            eng.wait_ge(s["vectors_ready"], 1)
            lruT = pvT[:, V_LAM:V_LAM + KC]
            eng.scalar_tensor_tensor(out=sp[:, 0, :], in0=lruT, scalar=-1.0, in1=lruT, op0=ALU.mult,
                                     op1=ALU.max).then_inc(s["softplus_in"], 1)
            link(eng.tensor_scalar(sp[:, 6, :], lruT, -1.0, 0.0, ALU.mult, ALU.max))
            eng.wait_ge(s["softplus_exp"], 1)
            link(eng.tensor_scalar(sp[:, 2, :], sp[:, 1, :], 2.0, None, ALU.add))
            link(eng.reciprocal(sp[:, 3, :], sp[:, 2, :]))
            link(eng.tensor_tensor(sp[:, 2, :], sp[:, 1, :], sp[:, 3, :], ALU.mult))
            link(eng.tensor_tensor(sp[:, 3, :], sp[:, 2, :], sp[:, 2, :], ALU.mult))
            link(eng.tensor_scalar(sp[:, 7, :], sp[:, 3, :], 1.0 / 19, None, ALU.mult))
            for k in range(8, 0, -1):
                link(eng.scalar_tensor_tensor(out=sp[:, 7, :], in0=sp[:, 7, :], scalar=1.0 / (2 * k + 1),
                                              in1=sp[:, 3, :], op0=ALU.add, op1=ALU.mult))
            link(eng.scalar_tensor_tensor(out=sp[:, 7, :], in0=sp[:, 7, :], scalar=1.0, in1=sp[:, 2, :],
                                          op0=ALU.add, op1=ALU.mult))
            link(eng.scalar_tensor_tensor(out=sp[:, 7, :], in0=sp[:, 7, :], scalar=2.0, in1=sp[:, 6, :],
                                          op0=ALU.mult, op1=ALU.add))
            link(eng.tensor_scalar(sp[:, 4, :], sp[:, 7, :], -RGLRU_C, None, ALU.mult))
            eng.tensor_scalar(sp[:, 5, :], sp[:, 7, :], RGLRU_C, None, ALU.mult).then_inc(s["softplus_ready"], 1)
            eng.wait_ge(s["lambda_vectors_loaded"], 64)
            for n in range(2):
                link(eng.tensor_tensor(lamv[:, 2 * n, :], lamv[:, 2 * n, :], lamv[:, 2 * n + 1, :], ALU.mult))
                eng.reduce_sum(lam[:, n:n + 1], lamv[:, 2 * n, :], AX_X).then_inc(s["lambda_sums_ready"], 1)
            eng.wait_ge(s["lambda_exps_ready"], 1)
            link(eng.tensor_tensor(lam[:, 4:5], lam[:, 3:4], lam[:, 2:3], ALU.subtract))
            link(eng.tensor_scalar(lam[:, 5:6], lam[:, 4:5], -LAM_INIT, None, ALU.add))
            link(eng.tensor_scalar(lam[:, 6:7], pvT[:, V_SUB:V_SUB + 1], 1.0 - LAM_INIT, None, ALU.mult))

            for n in range(4):
                eng.wait_ge(s["unit_out"], n + 1)
                for c in (2 * n, 2 * n + 1):
                    def tap(w):
                        return pvT[:, V_CONVW + w * KC + c:V_CONVW + w * KC + c + 1]
                    link(eng.tensor_scalar(xcT[:, c, :], xrT[:, c, :], tap(3), pvT[:, V_CONVB + c:V_CONVB + c + 1],
                                           ALU.mult, ALU.add))
                    for back in (1, 2, 3):
                        ins = eng.scalar_tensor_tensor(out=xcT[:, c, back:], in0=xrT[:, c, 0:T - back],
                                                       scalar=tap(3 - back), in1=xcT[:, c, back:],
                                                       op0=ALU.mult, op1=ALU.add)
                        if back < 3 or c % 2 == 0:
                            link(ins)
                ins.then_inc(s["conv_ready"], 1)
            eng.wait_ge(s["conv_ready"], 4)
            eng.wait_ge(s["gates_out"], KC)
            eng.wait_ge(s["gates_done"], KC)
            link(eng.tensor_tensor(iT[:, :, :], iT[:, :, :], xcT[:, :, :], ALU.mult))
            eng.wait_ge(s["decay_ready"], 2 * KC)
            link(eng.tensor_scalar(xcT[:, :, :], yrT[:, :, :], 1.0, None, ALU.add))
            link(eng.reciprocal(xcT[:, :, :], xcT[:, :, :]))
            eng.scalar_tensor_tensor(out=rT[:, :, :], in0=yrT[:, :, :], scalar=2.0, in1=xcT[:, :, :],
                                     op0=ALU.mult, op1=ALU.mult).then_inc(s["multiplier_in"], 1)
            eng.wait_ge(s["multiplier_ready"], 1)
            link(eng.tensor_tensor(iT[:, :, :], iT[:, :, :], rT[:, :, :], ALU.mult))
            for c in range(KC):
                ins = eng.tensor_tensor_scan(yrT[:, c, :], xrT[:, c, :], iT[:, c, :], 0.0, ALU.mult, ALU.add)
            ins.then_inc(s["scan_ready"], 1)

            def scores_in(h):
                b = h % 2
                eng.wait_ge(s["scores_done"], h + 1)
                s1 = sc[:, b, 0:512].rearrange("p (n k) -> p n k", n=2)
                s0 = sc[:, b, 512:768].rearrange("p (n k) -> p n k", n=2)
                ps0 = bank[4][:, 0:T].rearrange("p (n k) -> p n k", n=2)
                if h == 0:
                    eng.wait_ge(s["bias_tile_loaded"], 16)
                link(eng.tensor_tensor(s1, halves(bank[2 + b]), tb[:, h:h + 1, :].to_broadcast([P, 2, T]), ALU.add))
                link(eng.tensor_tensor(s0, ps0, tb[:, h:h + 1, P:T].to_broadcast([P, 2, P]), ALU.add))
                eng.tensor_reduce(st[:, b, 8:10], s1, AX_X, ALU.max)
                link(eng.tensor_reduce(st[:, b, 10:12], s0, AX_X, ALU.max))
                eng.tensor_scalar(st[:, b, 0:4], st[:, b, 8:12], -1.0, None, ALU.mult
                                  ).then_inc(s["scores_ready"], 1)

            def weights_in(h):
                b = h % 2
                eng.wait_ge(s["exps_done"], 4 * (h + 1))
                link(eng.reciprocal(st[:, b, 8:12], st[:, b, 4:8]))
                link(eng.tensor_scalar(st[:, b, 4:8], st[:, b, 8:12], lam[:, 5:6], None, ALU.mult))
                eng.tensor_scalar(sc[:, b, 256:512], sc[:, b, 256:512], st[:, b, 5:6], None, ALU.mult)
                link(eng.tensor_scalar(sc[:, b, 640:768], sc[:, b, 640:768], st[:, b, 7:8], None, ALU.mult))
                if h >= 1:
                    eng.wait_ge(s["weights_turned"], h)
                eng.scalar_tensor_tensor(out=wm[:, 0:256], in0=sc[:, b, 0:256], scalar=st[:, b, 8:9],
                                         in1=sc[:, b, 256:512], op0=ALU.mult, op1=ALU.add)
                eng.scalar_tensor_tensor(out=wm[:, 256:384], in0=sc[:, b, 512:640], scalar=st[:, b, 10:11],
                                         in1=sc[:, b, 640:768], op0=ALU.mult, op1=ALU.add
                                         ).then_inc(s["weights_ready"], 1)

            for step in range(12):
                if 1 <= step <= H:
                    weights_in(step - 1)
                if step < H:
                    scores_in(step)
                if step == 5:
                    eng.wait_ge(s["gelu_square"], 1)
                    link(eng.tensor_scalar(xcT[:, :, :], xcT[:, :, :], GELU_A, 1.0, ALU.mult, ALU.add))
                    eng.tensor_tensor(xcT[:, :, :], xcT[:, :, :], xrT[:, :, :], ALU.mult).then_inc(s["gelu_in"], 1)
                if step == 9:
                    eng.wait_ge(s["gelu_tanh"], 1)
                    link(eng.scalar_tensor_tensor(out=xcT[:, :, :], in0=xcT[:, :, :], scalar=1.0, in1=xrT[:, :, :],
                                                  op0=ALU.add, op1=ALU.mult))
                    eng.wait_ge(s["scan_ready"], 1)
                    eng.scalar_tensor_tensor(out=yrT[:, :, :], in0=xcT[:, :, :], scalar=0.5, in1=yrT[:, :, :],
                                             op0=ALU.mult, op1=ALU.mult).then_inc(s["rnn_ready"], 1)

            def gated(u):
                m, c, b = UNITS[u]
                f = 4 * c + 2 * b
                g = iT if m == "prnn" else rT
                eng.wait_ge(s["unit_done"], u + 1)
                ins = eng.scalar_tensor_tensor(out=g[:, f:f + 2, :], in0=g[:, f:f + 2, :], scalar=1.0,
                                               in1=halves(bank[u % 2]), op0=ALU.add, op1=ALU.mult)
                ins.then_inc(s["projection_out"], 1)
                if m == "patt":
                    eng.wait_ge(s["projection_out"], u + 1 - unit("prnn"))
                    eng.tensor_tensor(iT[:, f:f + 2, :], iT[:, f:f + 2, :], rT[:, f:f + 2, :], ALU.add
                                      ).then_inc(s["merged"], 1)

            eng.wait_ge(s["unit_out"], unit("g1", 3) + 1)
            gated(unit("prnn"))
            eng.wait_ge(s["heads_summed"], 4)
            for n in range(4):
                eng.tensor_scalar(orr[:, 2 * n:2 * n + 2, :], halves(bank[2 + n]), 1.0 / VD, EPS, ALU.mult, ALU.add
                                  ).then_inc(s["heads_ms"], 1)
            gated(unit("prnn", 1))
            eng.wait_ge(s["heads_std"], 1)
            link(eng.reciprocal(orr[:, :, :], orr[:, :, :]))
            eng.scalar_tensor_tensor(out=yaT[:, :, :], in0=oT[:, :, :], scalar=lam[:, 6:7], in1=orr[:, :, :],
                                     op0=ALU.mult, op1=ALU.mult).then_inc(s["att_ready"], 1)
            for u in range(unit("prnn", 2), unit("patt", 3) + 1):
                gated(u)
            eng.wait_ge(s["x_again_loaded"], 16 * TT)
            for u in range(unit("out"), unit("out", 3) + 1):
                _, c, t = UNITS[u]
                eng.wait_ge(s["unit_done"], u + 1)
                part = x2[:, t, c * CH:(c + 1) * CH]
                eng.scalar_tensor_tensor(out=part, in0=bank[u % 2][:, :], scalar=0.5, in1=part, op0=ALU.mult,
                                         op1=ALU.add).then_inc(s["mixed"], 1)

            def inverse_rms(squared, ms, std):
                eng.wait_ge(squared, 1)
                eng.tensor_scalar(small[:, 2:4], small[:, 0:2], 1.0 / D, EPS, ALU.mult, ALU.add).then_inc(ms, 1)
                eng.wait_ge(std, 1)
                link(eng.reciprocal(small[:, 6:8], small[:, 4:6]))

            inverse_rms(s["mixed_squared"], s["mixed_ms"], s["mixed_std"])
            eng.wait_ge(s["norm_rows_loaded"], 32)
            for t in range(TT):
                eng.scalar_tensor_tensor(out=h2[:, t, :], in0=x2[:, t, :], scalar=small[:, 6 + t:7 + t], in1=g2row,
                                         op0=ALU.mult, op1=ALU.mult).then_inc(s["ffn_ready"], 1)

            eng.wait_ge(s["logits_turned"], 1)
            eng.wait_ge(s["router_loaded"], 32)
            eng.tensor_scalar(r_logT, bank[0][0:NE, 0:T], brt[:, 0:1], None, ALU.add).then_inc(s["logits_biased"], 1)
            eng.wait_ge(s["logits_done"], 1)
            link(eng.tensor_copy(r_log, bank[1][:, 0:TT * NE].rearrange("p (t e) -> p t e", t=TT)))
            for t in range(TT):
                ins = eng.max(r_max[:, t, :], r_log[:, t, :])
            link(ins)
            eng.tensor_scalar(r_nmx, r_max[:, :, 0], -1.0, None, ALU.mult).then_inc(s["top_ready"], 1)
            fourth = r_max[:, :, TOPK - 1:TOPK].to_broadcast([P, TT, NE])
            eng.tensor_tensor(r_gt, r_log, fourth, ALU.is_gt)
            link(eng.tensor_tensor(r_eq, r_log, fourth, ALU.is_equal))
            for t in range(TT):
                eng.tensor_tensor_scan(r_rank[:, t, :], ones[:, 0:NE], r_eq[:, t, :], 0.0, ALU.mult, ALU.add)
            link(eng.tensor_reduce(r_ngt, r_gt, AX_X, ALU.add))
            link(eng.tensor_scalar(r_need, r_ngt, -1.0, float(TOPK), ALU.mult, ALU.add))
            for t in range(TT):
                ins = eng.scalar_tensor_tensor(out=r_rank[:, t, :], in0=r_rank[:, t, :], scalar=r_need[:, t:t + 1],
                                               in1=r_eq[:, t, :], op0=ALU.is_le, op1=ALU.mult)
            link(ins)
            link(eng.tensor_tensor(r_mask, r_gt, r_rank, ALU.add))
            eng.wait_ge(s["route_exps"], TT)
            link(eng.tensor_tensor(r_exp, r_exp, r_mask, ALU.mult))
            link(eng.tensor_reduce(r_sum, r_exp, AX_X, ALU.add))
            link(eng.reciprocal(r_inv, r_sum))
            for t in range(TT):
                eng.tensor_scalar(r_gate[:, t, :], r_exp[:, t, :], r_inv[:, t:t + 1], None, ALU.mult
                                  ).then_inc(s["route_ready"], 1)
            eng.wait_ge(s["route_out"], 1)
            link(eng.tensor_tensor_scan(inclT, ones[0:NE, 0:T], maskT, 0.0, ALU.mult, ALU.add))
            link(eng.tensor_tensor(slotT, inclT, maskT, ALU.mult))
            eng.tensor_scalar(slotT, slotT, -1.0, None, ALU.add)
            total = inclT[:, T - 1:T]
            link(eng.tensor_scalar(novf, total, float(JB), None, ALU.is_gt))
            for b in range(2, T // JB):
                ins = eng.scalar_tensor_tensor(out=novf, in0=total, scalar=float(b * JB), in1=novf, op0=ALU.is_gt,
                                               op1=ALU.add)
                if b < T // JB - 1:
                    link(ins)
            ins.then_inc(s["overflow_ready"], 1)
            eng.wait_ge(s["ends_done"], 1)
            link(eng.tensor_copy(ends, bank[3][0:NE, 0:1]))
            link(eng.tensor_tensor(starts, ends, novf, ALU.subtract))
            more = iota_job[:, 0:JOBS - NE]
            link(eng.tensor_scalar(owork, more, ends, None, ALU.is_lt))
            eng.wait_ge(s["job_tiles_cleared"], 2)
            eng.tensor_copy(ohj[0:NE, 0:NE], ident[0:NE, 0:NE])
            eng.memset(block64[:, 0:NE], 0.0)
            link(eng.scalar_tensor_tensor(out=ohj[0:NE, NE:JOBS], in0=more, scalar=starts, in1=owork, op0=ALU.is_ge,
                                          op1=ALU.mult))
            link(eng.tensor_scalar(owork, more, starts, -float(JB), ALU.subtract, ALU.mult))
            eng.scalar_tensor_tensor(out=block64[:, NE:JOBS], in0=owork, scalar=-float(JB),
                                     in1=ohj[0:NE, NE:JOBS], op0=ALU.add, op1=ALU.mult).then_inc(s["jobs_ready"], 1)
            eng.wait_ge(s["job_columns_done"], 1)
            eng.tensor_copy(arena[:, 4, 1024:1024 + 2 * TT * JOBS], bank[0][:, 0:2 * TT * JOBS]
                            ).then_inc(s["job_columns_ready"], 1)
            eng.tensor_copy(jobi[0:1, 0:JOBS], bank[0][0:1, 256:256 + JOBS])
            eng.tensor_scalar(jobi[0:1, JOBS:JOBS + 1], bank[0][0:1, 256 + JOBS:257 + JOBS], float(NE), None,
                              ALU.add).then_inc(s["job_table_ready"], 1)

            def select(n):
                for t in range(TT):
                    ins = eng.tensor_scalar(sel[:, t, :], iota_slot[:, 0:JB], jcol[:, t, n], None, ALU.is_equal)
                ins.then_inc(job["selection"], 1)

            def expert_onehot(n):
                eng.tensor_scalar(ohb, ones[:, 0:JB], ohj[:, n], None, ALU.mult).then_inc(job["expert_onehot"], 1)

            eng.sem_inc(job["activation"], 1)
            eng.sem_inc(job["up_clamped"], 1)
            eng.wait_ge(s["job_columns_ready"], 1)
            select(slice(0, 1))
            expert_onehot(slice(0, 1))
            eng.wait_ge(s["job_table_ready"], 1)
            jobs = eng.value_load(jobi[0:1, JOBS:JOBS + 1], min_val=NE, max_val=JOBS - 1)
            with eng.Fori(0, jobs) as j:
                eng.wait_ge(job["gathered"], j + 1)
                select(bass.ds(j + 1, 1))
                eng.wait_ge(job["scatter_turned"], j + 1)
                for t in range(TT):
                    ins = eng.tensor_scalar(selw[:, t, :], iota_slot[:, :], jcol[:, t, bass.ds(j, 1)],
                                            gcol[:, t, bass.ds(j, 1)], ALU.is_equal, ALU.mult)
                ins.then_inc(job["weighted_selection"], 1)
                eng.wait_ge(job["gate_done"], j + 1)
                eng.tensor_scalar(gm, bank[0][:, :], LIMIT, None, ALU.min).then_inc(job["gate_clamped"], 1)
                eng.wait_ge(job["up_done"], j + 1)
                eng.tensor_scalar(uc, bank[1][:, :], LIMIT, -LIMIT, ALU.min, ALU.max).then_inc(job["up_clamped"], 1)
                eng.wait_ge(job["gate_clamped"], j + 1)
                eng.wait_ge(job["up_clamped"], j + 2)
                eng.scalar_tensor_tensor(out=uc, in0=uc, scalar=1.0, in1=gm, op0=ALU.add, op1=ALU.mult
                                         ).then_inc(job["product"], 1)
                eng.wait_ge(job["product"], j + 1)
                eng.wait_ge(job["sigmoid"], j + 1)
                eng.wait_ge(job["activation_turned"], j + 1)
                eng.tensor_tensor(av, uc, sg, ALU.mult).then_inc(job["activation"], 1)
                expert_onehot(bass.ds(j + 1, 1))
            eng.wait_ge(job["scattered"], jobs + 1)
            for t in range(TT):
                for h in range(2):
                    part = x2[:, t, h * CH:(h + 1) * CH]
                    eng.tensor_tensor(part, bank[4 + 2 * t + h][:, :], part, ALU.add).then_inc(s["result_ready"], 1)
            inverse_rms(s["result_squared"], s["result_ms"], s["result_std"])
            for t in range(TT):
                eng.scalar_tensor_tensor(out=h2[:, t, :], in0=x2[:, t, :], scalar=small[:, 6 + t:7 + t], in1=gfrow,
                                         op0=ALU.mult, op1=ALU.mult).then_inc(s["fin"], 1)

        @block.tensor
        def _(eng):
            eng.wait_ge(s["identity_ready"], 2)
            eng.wait_ge(s["vectors_loaded"], 16 * 7)
            eng.transpose(bank[7][:, 0:NV], pv[:, :], ident[0:NV, 0:NV]).then_inc(s["vectors_turned"], 1)
            eng.wait_ge(s["constants_ready"], 1)
            eng.wait_ge(s["rel_loaded"], 16)
            eng.wait_ge(s["onehot_loaded"], 16)
            eng.matmul(bank[6][0:H, 0:DIFFS], rel[:, :], onehot, start=True, stop=True
                       ).then_inc(s["bias_vector_done"], 1)

            def turn(src, banks, ready, turned):
                for n in range(4):
                    for c in (2 * n, 2 * n + 1):
                        for t in range(TT):
                            if n == 0 and c == 0:
                                eng.wait_ge(ready, t + 1)
                            ins = eng.transpose(bank[banks[n]][:, (c % 2) * T + t * P:(c % 2) * T + (t + 1) * P],
                                                src[:, t, c * P:(c + 1) * P], ident[:, :])
                    ins.then_inc(turned, 1)

            turn(hn, (2, 3, 4, 5), s["x_normed"], s["norm_turned"])
            eng.wait_ge(s["norm_ready"], KC)

            def product(u, rhs=None, lhsT=None):
                m, c, b = UNITS[u]
                i = u // 2
                if b == 0:
                    eng.wait_ge(chunk_loaded[i % 2], 16 * (i // 2 + 1))
                if u >= 2:
                    if u - 2 < unit("prnn"):
                        eng.wait_ge(s["unit_out"], u - 1)
                    elif u - 2 < unit("out"):
                        eng.wait_ge(s["projection_out"], u - 1 - unit("prnn"))
                    else:
                        eng.wait_ge(s["mixed"], u - 1 - unit("out"))
                w = wst[:, i % 2]
                ps = bank[u % 2]
                if rhs is not None:
                    for n in range(2):
                        for k in range(KC):
                            ins = eng.matmul(ps[:, n * T:(n + 1) * T], w[:, k, (2 * b + n) * P:(2 * b + n + 1) * P],
                                             rhs[:, k, :], start=(k == 0), stop=(k == KC - 1))
                else:
                    for k in range(KC):
                        ins = eng.matmul(ps[:, :], lhsT[:, k, b * P:(b + 1) * P], w[:, k, :],
                                         start=(k == 0), stop=(k == KC - 1))
                ins.then_inc(s["unit_done"], 1)
                if b == 1:
                    eng.wait_ge(s["unit_done"], u + 1)
                    eng.sem_inc(s["chunk_used"], 1)

            for n in range(4):
                product(unit("xr") + n, rhs=hT)
            for n in range(4):
                product(unit("v") + n, lhsT=hT)
            eng.wait_ge(s["block_diagonals_loaded"], 64)
            for n in range(KC):
                eng.wait_ge(s["conv_ready"], min(n, 3) + 1)
                if n >= 6:
                    eng.wait_ge(s["gates_out"], n - 5)
                for b in range(2):
                    g, c = n // 4, 2 * (n % 4) + b
                    ins = eng.matmul(bank[2 + n % 6][:, b * T:(b + 1) * T], blkd[:, g * KC + c, :], xcT[:, c, :],
                                     start=True, stop=True)
                ins.then_inc(s["gates_done"], 1)
            for n in range(4):
                product(unit("q") + n, rhs=hT)
            for n in range(4):
                product(unit("k") + n, rhs=hT)
            eng.wait_ge(s["gates_out"], KC)

            def scores(h):
                if h == 0:
                    eng.wait_ge(s["unit_out"], unit("k", 3) + 1)
                if h >= 1:
                    eng.wait_ge(s["scores_ready"], h)
                for n in range(2):
                    eng.matmul(bank[2 + h % 2][:, n * T:(n + 1) * T], qz[n][:, h, P:T], kT[:, h, :],
                               start=True, stop=True)
                for n in range(2):
                    ins = eng.matmul(bank[4][:, n * P:(n + 1) * P], qz[n][:, h, 0:P], kT[:, h, 0:P], start=True, stop=True)
                ins.then_inc(s["scores_done"], 1)

            def turn_weights(h):
                eng.wait_ge(s["weights_ready"], h + 1)
                if h >= 1:
                    eng.wait_ge(s["weights_out"], h)
                eng.transpose(bank[5][:, 0:P], wm[:, 256:384], ident[:, :])
                eng.transpose(bank[5][:, P:2 * P], wm[:, 0:P], ident[:, :])
                eng.transpose(bank[5][:, 2 * P:3 * P], wm[:, P:2 * P], ident[:, :]).then_inc(s["weights_turned"], 1)

            def head(h):
                eng.wait_ge(s["weights_out"], h + 1)
                if h >= 1:
                    eng.wait_ge(s["head_out"], h)
                v = [vS[:, t, h * VD:(h + 1) * VD] for t in range(TT)]
                eng.matmul(bank[6][:, 0:P], v[0], wT[:, 0:P], start=True, stop=True)
                eng.matmul(bank[6][:, P:T], v[0], wT[:, P:T], start=True, stop=False)
                eng.matmul(bank[6][:, P:T], v[1], wT[:, T:T + P], start=False, stop=True
                           ).then_inc(s["head_done"], 1)

            for step in range(12):
                product(unit("gr") + step, rhs=hT)
                if step < H:
                    scores(step)
                if 1 <= step <= H:
                    turn_weights(step - 1)
                if 2 <= step <= H + 1:
                    head(step - 2)
            eng.wait_ge(s["rnn_ready"], 1)
            product(unit("prnn"), rhs=yrT)
            eng.wait_ge(s["heads_squared"], 1)
            for n in range(4):
                eng.matmul(bank[2 + n][:, :], ones[:, 0:P], osq[:, 2 * n:2 * n + 2, :].rearrange("p a b -> p (a b)"),
                           start=True, stop=True).then_inc(s["heads_summed"], 1)
            for n in range(1, 4):
                product(unit("prnn", n), rhs=yrT)
            eng.wait_ge(s["att_ready"], 1)
            for n in range(4):
                product(unit("patt", n), rhs=yaT)
            eng.wait_ge(s["merged"], 4)
            for n in range(4):
                product(unit("out", n), lhsT=iT)

            eng.wait_ge(s["mixed"], 4)
            turn(h2, (0, 1, 2, 3), s["ffn_ready"], s["ffn_turned"])
            eng.wait_ge(s["router_loaded"], 32)
            for k in range(KC):
                if k % 2 == 0:
                    eng.wait_ge(s["ffn_turned_out"], 4 if k == 0 else k // 2 + 1)
                ins = eng.matmul(bank[0][0:NE, 0:T], wr[:, k, :], hfT[:, k, :], start=(k == 0), stop=(k == KC - 1))
            ins.then_inc(s["logits_turned"], 1)
            eng.wait_ge(s["logits_biased"], 1)
            for t in range(TT):
                ins = eng.transpose(bank[1][:, t * NE:(t + 1) * NE], r_logT[:, t * P:(t + 1) * P], ident[0:NE, 0:NE])
            ins.then_inc(s["logits_done"], 1)
            eng.wait_ge(s["route_ready"], TT)
            for n, src in enumerate((r_mask, r_gate)):
                for t in range(TT):
                    ins = eng.transpose(bank[2][0:NE, n * T + t * P:n * T + (t + 1) * P], src[:, t, :], ident[:, :])
            ins.then_inc(s["route_turned"], 1)
            eng.wait_ge(s["overflow_ready"], 1)
            eng.wait_ge(s["constants_ready"], 7)
            eng.matmul(bank[3][0:NE, 0:1], tri[:, :], novf, start=True, stop=True).then_inc(s["ends_done"], 1)
            eng.wait_ge(s["jobs_ready"], 1)
            for t in range(TT):
                o = t * JOBS
                eng.matmul(bank[0][:, o:o + JOBS], slotT[:, t * P:(t + 1) * P], ohj[0:NE, :], start=True, stop=False)
                eng.matmul(bank[0][:, o:o + JOBS], ones[0:NE, 0:P], block64, start=False, stop=True)
            for t in range(TT):
                o = (TT + t) * JOBS
                eng.matmul(bank[0][:, o:o + JOBS], gateT[:, t * P:(t + 1) * P], ohj[0:NE, :], start=True, stop=True)
            eng.matmul(bank[0][0:1, 256:256 + JOBS], ecol[:, :], ohj[0:NE, :], start=True, stop=True)
            eng.matmul(bank[0][0:1, 256 + JOBS:257 + JOBS], ones[0:NE, 0:1], novf, start=True, stop=True
                       ).then_inc(s["job_columns_done"], 1)
            eng.wait_ge(s["bias_rows_loaded"], 48)
            for t in range(TT):
                for h in range(2):
                    eng.matmul(bank[4 + 2 * t + h][:, :], gateT[:, t * P:(t + 1) * P], bdrow[:, h * CH:(h + 1) * CH],
                               start=True, stop=True, skip_group_check=True)

            def pair(ps, lhsT, w, **flags):
                for h in range(2):
                    ins = eng.matmul(ps[h * JB:(h + 1) * JB, :], lhsT, w[:, h * CH:(h + 1) * CH], **flags)
                return ins

            def block_of(turned, k):
                return turned[:, k % 4, (k // 4) * JB:(k // 4 + 1) * JB]

            def gather():
                for t in range(TT):
                    ins = pair(bank[2], sel[:, t, :], h2[:, t, :], start=(t == 0), stop=(t == TT - 1))
                ins.then_inc(job["gathered"], 1)

            def turn_gather():
                for c in range(4):
                    ins = eng.transpose(bank[2][:, c * P:(c + 1) * P], xg[:, c * P:(c + 1) * P], ident[:, :])
                ins.then_inc(job["gather_turned"], 1)

            eng.sem_inc(job["scattered"], 1)
            eng.sem_inc(job["scatter_turned"], 1)
            eng.sem_inc(job["activation_turned"], 1)
            eng.wait_ge(job["selection"], 1)
            gather()
            eng.wait_ge(job["gather_out"], 1)
            turn_gather()
            eng.wait_ge(s["job_table_ready"], 1)
            jobs = eng.value_load(jobi[0:1, JOBS:JOBS + 1], min_val=NE, max_val=JOBS - 1)
            with eng.Fori(0, jobs) as j:
                eng.wait_ge(job["input"], j + 1)
                eng.wait_ge(job["expert_onehot"], j + 1)
                eng.wait_ge(job["activation_out"], j + 1)
                for m, ps, w, row, ready in (("gate", bank[0], WG, 0, "gate_done"), ("up", bank[1], WU, 1, "up_done")):
                    if m == "up":
                        eng.wait_ge(job["up_clamped"], j + 1)
                    pair(ps, ohb, brow[:, row, :], start=True, stop=False)
                    for q in range(NQ):
                        eng.wait_ge(loaded[m][q], j * 16 + 16)
                        for k in (2 * q, 2 * q + 1):
                            ins = pair(ps, block_of(xgT, k), w[:, k, :], start=False, stop=(k == KC - 1))
                        if q < NQ - 1:
                            ins.then_inc(used[m], 1)
                        else:
                            ins.then_inc(job[ready], 1)
                            eng.wait_ge(job[ready], j + 1)
                            eng.sem_inc(used[m], 1)
                eng.wait_ge(job["selection"], j + 2)
                gather()
                eng.wait_ge(job["weighted_selection"], j + 1)
                eng.wait_ge(job["output_out"], j + 1)
                for t in range(TT):
                    ins = eng.transpose(bank[3][:, t * P:(t + 1) * P], selw[:, t, :], ident[:, :])
                ins.then_inc(job["scatter_turned"], 1)
                eng.wait_ge(job["gather_out"], j + 2)
                turn_gather()
                eng.wait_ge(job["activation"], j + 2)
                for c in range(4):
                    ins = eng.transpose(bank[0][:, c * P:(c + 1) * P], av[:, c * P:(c + 1) * P], ident[:, :])
                ins.then_inc(job["activation_turned"], 1)
                eng.wait_ge(job["scatter_ready"], j + 1)
                eng.wait_ge(job["activation_out"], j + 2)
                for q in range(NQ):
                    eng.wait_ge(loaded["down"][q], j * 16 + 16)
                    for k in (2 * q, 2 * q + 1):
                        ins = pair(bank[3], block_of(avT, k), WD[:, k, :], start=(k == 0), stop=(k == KC - 1))
                    if q < NQ - 1:
                        ins.then_inc(used["down"], 1)
                    else:
                        ins.then_inc(job["down_done"], 1)
                        eng.wait_ge(job["down_done"], j + 1)
                        eng.sem_inc(used["down"], 1)
                eng.wait_ge(job["output_out"], j + 2)
                for t in range(TT):
                    for h in range(2):
                        ins = eng.matmul(bank[4 + 2 * t + h][:, :], swz[:, h, t, :], ys, start=False, stop=True,
                                         skip_group_check=True)
                ins.then_inc(job["scattered"], 1)


_INS = ["x", "norm_mix_g", "w_in", "conv_w", "conv_b", "w_rg_a", "b_rg_a", "w_rg_x", "b_rg_x", "lru_lambda",
        "diff_lambda_q1", "diff_lambda_k1", "diff_lambda_q2", "diff_lambda_k2", "subln_g", "rel_bias_table",
        "w_proj_rnn", "w_proj_att", "w_out", "norm_ffn_g", "w_router", "b_router", "w_gate_e", "b_gate_e",
        "w_up_e", "b_up_e", "w_down_e", "b_down_e", "norm_final_g"]


def kernel(**inputs):
    from concourse import bacc
    from concourse.bass_utils import run_bass_kernel_spmd

    nc = bacc.Bacc("TRN2", target_bir_lowering=False, num_devices=1)
    arrays, args = {}, {}
    for name in _INS:
        a = np.ascontiguousarray(inputs[name])
        arrays[f"in_{name}"] = a
        args[name] = nc.dram_tensor(f"in_{name}", a.shape, mybir.dt.from_np(a.dtype), kind="ExternalInput").ap()
    arrays["in_bucket_onehot"] = bucket_onehot()
    args["bucket_onehot"] = nc.dram_tensor("in_bucket_onehot", (NBUCKET + 1, DIFFS), F32, kind="ExternalInput").ap()
    result = nc.dram_tensor("out_0", (1, T, D), F32, kind="ExternalOutput").ap()
    hybrid_block(nc, args, result)
    r = run_bass_kernel_spmd(nc, [arrays], core_ids=[0])
    return r.results[0]["out_0"]
```

```python
import math
from contextlib import ExitStack

import numpy as np

import concourse.bass as bass
from concourse import mybir

F32 = mybir.dt.float32
I32 = mybir.dt.int32
ALU = mybir.AluOpType
ACT = mybir.ActivationFunctionType
AX_X = mybir.AxisListType.X

P = 128
D = 1024
KC = D // P
T = 256
TT = T // P
H = 8
HD = 64
VD = 128
RB = 64
NBUCKET = 32
NE = 32
TOPK = 4
JB = 64
JOBS = 50
MORE = JOBS - NE
CH = 512
NQ = 4
DIFFS = 384
EPS = 1e-6
NEG = -1e30
LIMIT = 7.0
SWIGLU_ALPHA = 1.702
RGLRU_C = 8.0
LAM_INIT = 0.8 - 0.6 * math.exp(-0.3 * 0)
GELU_A = 0.044715
GELU_B = math.sqrt(2.0 / math.pi)

V_CONVW, V_CONVB, V_BA, V_BX, V_LAM, V_SUB = 0, 32, 40, 48, 56, 64
NV = 65

MIX = ["xr", "v", "q", "k", "gr", "g0", "g1"]
COLUMN = {"xr": 0, "gr": D, "q": 2 * D, "k": 3 * D, "v": 4 * D, "g0": 5 * D, "g1": 6 * D}
STREAM = [(m, c) for m in MIX + ["prnn", "patt", "out"] for c in range(D // CH)]
UNITS = ([(m, c, b) for m, c in STREAM if m != "out" for b in range(2)]
         + [("out", c, t) for t in range(TT) for c in range(D // CH)])


def unit(name, n=0):
    return [i for i, (m, _, _) in enumerate(UNITS) if m == name][n]


def units_through(i):
    return max(u for u, (m, c, _) in enumerate(UNITS) if (m, c) == STREAM[i]) + 1


def bucket_onehot():
    out = np.zeros((NBUCKET + 1, DIFFS), np.float32)
    half = NBUCKET // 2
    for m in range(DIFFS):
        n = T - 1 - m
        if n < 0:
            b = NBUCKET
        elif n < half:
            b = n
        else:
            b = min(half + int(math.log(n / half) / math.log(128 / half) * half), NBUCKET - 1)
        out[b, m] = 1.0
    return out


SIGNALS = """gain_loaded gain_turned gain_ready x_loaded_0 x_loaded_1 vectors_loaded
block_diagonals_cleared block_diagonals_loaded onehot_loaded
rel_loaded lambda_vectors_loaded bias_vector_stored bias_tile_loaded router_loaded ffn_norm_loaded
final_norm_loaded
bias_rows_loaded x_again_loaded out_stored
identity_ready constants_ready query_zeros_ready bias_rows_cleared gates_turned_cleared
down_biases_cleared job_tiles_cleared
x_squared x_ms x_std x_normed vectors_turned vectors_ready norm_turned norm_low_ready norm_high_ready
bias_vector_done bias_vector_ready lambda_sums_ready lambda_exps_ready softplus_in
softplus_exp softplus_ready conv_ready gates_done gates_out decay_ready multiplier_in
multiplier_ready scan_ready gelu_square gelu_in gelu_tanh rnn_ready
scores_done scores_ready exps_done weights_ready weights_turned weights_out head_done head_out
heads_squared heads_summed heads_ms heads_std att_ready merged mixed
unit_done unit_out projection_out
mixed_squared mixed_gained mixed_ms mixed_std mixed_inverse ffn_low ffn_high ffn_turned ffn_low_out ffn_high_out
logits_turned logits_biased logits_done top_ready route_exps mask_ready mask_turned weight_ready
weight_turned weight_out slots_ready slot_columns_done slot_columns_ready overflow_ready ends_done
jobs_ready late_columns_done job_table_ready
result_ready result_squared result_gained result_ms result_std result_inverse fin_low fin_high""".split()

JOB_SIGNALS = """selection gathered gather_out gather_turned input expert_onehot gate_done gate_clamped
sigmoid gate_ready up_done up_clamped activation weighted_selection scatter_turned scatter_ready
activation_turned activation_out down_done output_half_out output_out scattered_first scattered""".split()


def hybrid_block(nc, A, out):
    with ExitStack() as ctx:
        def sb(name, shape, dt=F32):
            return ctx.enter_context(nc.sbuf_tensor(name, shape, dt))

        def sem(name):
            return ctx.enter_context(nc.semaphore(name))

        WG = sb("w_gate_sb", [P, KC, D])
        WU = sb("w_up_sb", [P, KC, D])
        WD = sb("w_down_sb", [P, KC, D])
        wst = WD[:, :, :].rearrange("p a n -> p (a n)").rearrange("p (s k n) -> p s k n", s=2, k=KC)
        arena = sb("arena", [P, 12, 2048])

        def tile(n, a=KC, off=0, size=2048):
            return arena[:, n, off:off + size].rearrange("p (a b) -> p a b", a=a)

        hT = tile(0)
        hn = tile(1, TT)
        oT = tile(1)
        xrT = tile(2)
        xcT = tile(3)
        rT = tile(4)
        iT = tile(5)
        yrT = tile(6)
        onehot = arena[0:NBUCKET + 1, 6, 0:DIFFS]
        bias_vec = arena[0:H, 6, DIFFS:2 * DIFFS]
        blkd = tile(7, 16)
        qz = [tile(7), tile(8)]
        osq = tile(7)
        orr = tile(8)
        kT = tile(9)
        yaT = tile(9)
        vS = tile(10, TT)
        x2 = tile(10, TT)
        tb = tile(11)
        WG_ODD = arena[:, 0:4, :].rearrange("p a n -> p (a n)").rearrange("p (k n) -> p k n", k=KC)
        scat = arena[:, 4, 0:512].rearrange("p (h t n) -> p h t n", h=2, t=TT)
        sel = tile(4, TT, 512, TT * JB)
        selw = tile(4, TT, 640, TT * 2 * JB)
        ohb = arena[:, 4, 896:896 + JB]
        jcol = tile(4, TT, 1024, TT * JOBS)
        gcol = tile(4, TT, 1024 + TT * JOBS, TT * JOBS)
        ohj = arena[:, 4, 1280:1280 + JOBS]
        junk = arena[:, 4, 1408:1408 + CH]
        gfrow = arena[:, 5, 0:D]
        brow = arena[:, 6, :].rearrange("p (m n) -> p m n", m=2)
        h2 = tile(7, TT)
        hfT = tile(8)
        xg = arena[:, 8, 0:512]
        xgT = [tile(8, 4, 512, 512), tile(5, 4, D, 512)]
        gm, uc = arena[:, 8, 1024:1536], arena[:, 8, 1536:2048]
        g2row = arena[:, 9, 0:D]
        bdrow = arena[:, 9, D:2 * D]
        sg, av = arena[:, 11, 0:512], arena[:, 11, 512:1024]
        avT = tile(11, 4, 1024, 512)
        ys = [arena[:, 11, 1536:2048], arena[:, 5, 1536:2048]]

        def rt(off, *shape):
            ap = arena[:, 11, off:off + math.prod(shape)]
            return ap.rearrange("p (a b) -> p a b", a=shape[0]) if len(shape) == 2 else ap
        r_log, r_gt, r_eq, r_rank, r_exp = (rt(64 * n, TT, NE) for n in range(5))
        r_mask, r_gate = rt(320, TT, NE), rt(384, TT, NE)
        r_max, r_nmx, r_ngt, r_need = rt(448, TT, 8), rt(464, TT), rt(466, TT), rt(468, TT)
        r_sum, r_inv = rt(470, TT), rt(472, TT)
        r_logT = arena[0:NE, 11, 512:512 + T]
        gateT = arena[:, 11, 768:768 + T]
        inclT, slotT = arena[0:NE, 11, 1280:1280 + T], arena[0:NE, 11, 1536:1536 + T]
        novf, ends, starts = (arena[0:NE, 11, 1792 + n:1793 + n] for n in range(3))
        extra, pairs = arena[0:1, 11, 1796:1797], arena[0:1, 11, 1797:1798]
        block64, owork = arena[0:NE, 11, 1800:1800 + MORE], arena[0:NE, 11, 1820:1820 + MORE]
        under = arena[0:1, 11, 1840:1840 + MORE // 2]

        ident = sb("ident", [P, P])
        ones = sb("ones", [P, T])
        iota_slot = sb("iota_slot", [P, 2 * JB])
        iota_job = sb("iota_job", [NE, JOBS])
        tri = sb("tri", [NE, NE])
        ecol = sb("ecol", [NE, 1])
        gain = sb("gain", [KC, P])
        gainT = sb("gainT", [P, KC])
        pv = sb("pv", [NV, P])
        pvT = sb("pvT", [P, NV])
        sp = sb("sp", [P, 8, KC])
        wr = sb("wr", [P, KC, NE])
        brt = sb("brt", [NE, 1])
        rel = sb("rel", [NBUCKET + 1, H])
        lamv = sb("lamv", [P, 4, HD])
        lam = sb("lam", [P, 8])
        small = sb("small", [P, TT, 8])
        sc = sb("sc", [P, 2, 768])
        wm = sb("wm", [P, 384])
        wT = sb("wT", [P, 384])
        st = sb("st", [P, 2, 12])
        jobi = sb("jobi", [1, 64], I32)

        bank = [ctx.enter_context(nc.psum_tensor(f"bank{i}", [P, 512], F32)) for i in range(8)]

        def halves(ps):
            return ps[:, :].rearrange("p (a b) -> p a b", a=2)

        def quarters(ps):
            return ps[:, :].rearrange("p (a b) -> p a b", a=4)

        head_size = P * (DIFFS + 1)
        scratch = nc.dram_tensor("bias_scratch", (H, head_size), F32, kind="Internal").ap()

        s = {n: sem(n) for n in SIGNALS}
        job = {n: sem(f"job_{n}") for n in JOB_SIGNALS}
        chunk_loaded = [sem("chunk_loaded_0"), sem("chunk_loaded_1")]
        loaded = {m: [sem(f"{m}_loaded_{q}") for q in range(NQ)] for m in ("gate", "gate_odd", "up", "down")}
        used = {m: sem(f"{m}_used") for m in ("gate", "up", "down")}
        dve_order = sem("dve_order")
        W_EXP = {"gate": (A["w_gate_e"], WG), "gate_odd": (A["w_gate_e"], WG_ODD), "up": (A["w_up_e"], WU), "down": (A["w_down_e"], WD)}

        def broadcast(a, shape):
            return bass.AP(a.tensor, a.offset, [[0, P], [1, shape]])

        block = ctx.enter_context(nc.Block())

        @block.sync
        def _(eng):
            for t in range(TT):
                eng.dma_start(hn[:, t, :], A["x"][0, t * P:(t + 1) * P, :]).then_inc(s[f"x_loaded_{t}"], 16)
            eng.dma_start(gain[:, :], A["norm_mix_g"].rearrange("l (c p) -> (l c) p", p=P)).then_inc(s["gain_loaded"], 16)

            def chunk(i):
                m, c = STREAM[i]
                if m in COLUMN:
                    w, col = A["w_in"][0], COLUMN[m] + c * CH
                else:
                    w, col = A[{"prnn": "w_proj_rnn", "patt": "w_proj_att", "out": "w_out"}[m]][0], c * CH
                if i >= 2:
                    eng.wait_ge(s["unit_done"], units_through(i - 2))
                eng.dma_start(wst[:, i % 2], w[:, col:col + CH].rearrange("(k p) n -> p k n", p=P)
                              ).then_inc(chunk_loaded[i % 2], 16)

            chunk(0)
            for r, a in ((V_CONVB, A["conv_b"]), (V_LAM, A["lru_lambda"])):
                eng.dma_start(pv[r:r + KC, :], a.rearrange("l (c p) -> (l c) p", p=P)).then_inc(s["vectors_loaded"], 16)
            eng.dma_start(pv[V_CONVW:V_CONVW + 4 * KC, :], A["conv_w"].rearrange("l w (c p) -> (l w c) p", p=P)
                          ).then_inc(s["vectors_loaded"], 16)
            for r, a in ((V_BA, A["b_rg_a"]), (V_BX, A["b_rg_x"])):
                eng.dma_start(pv[r:r + KC, :], a.rearrange("l (c b) d -> (l c) (b d)", b=2)
                              ).then_inc(s["vectors_loaded"], 16)
            eng.dma_start(pv[V_SUB:V_SUB + 1, :], A["subln_g"]).then_inc(s["vectors_loaded"], 16)
            eng.dma_start(rel[0:NBUCKET, :], A["rel_bias_table"]).then_inc(s["rel_loaded"], 16)
            eng.dma_start(onehot, A["bucket_onehot"]).then_inc(s["onehot_loaded"], 16)
            chunk(1)
            for n, name in enumerate(["diff_lambda_q1", "diff_lambda_k1", "diff_lambda_q2", "diff_lambda_k2"]):
                eng.dma_start(lamv[:, n, :], broadcast(A[name], HD)).then_inc(s["lambda_vectors_loaded"], 16)
            eng.wait_ge(s["block_diagonals_cleared"], 1)
            for g, name in enumerate(["w_rg_a", "w_rg_x"]):
                for half in range(2):
                    src = A[name][0].rearrange("(n b) c d -> b c n d", b=2)[half]
                    eng.dma_start(blkd[half * RB:(half + 1) * RB, g * KC:(g + 1) * KC, half * RB:(half + 1) * RB],
                                  src).then_inc(s["block_diagonals_loaded"], 16)
            eng.dma_start(wr[:, :, :], A["w_router"][0].rearrange("(k p) e -> p k e", p=P)
                          ).then_inc(s["router_loaded"], 16)
            eng.dma_start(brt[:, :], A["b_router"].rearrange("l e -> e l")).then_inc(s["router_loaded"], 16)
            eng.wait_ge(s["bias_vector_ready"], 1)
            eng.dma_start(scratch.rearrange("h (q m) -> h q m", q=P)[:, :, 0:DIFFS],
                          bias_vec.rearrange("h (a m) -> h a m", a=1).to_broadcast([H, P, DIFFS])
                          ).then_inc(s["bias_vector_stored"], 16)
            chunk(2)
            eng.wait_ge(s["bias_vector_stored"], 16)
            back = bass.AP(scratch.tensor, scratch.offset + P - 1, [[DIFFS, P], [head_size, H], [1, T]])
            eng.dma_start(tb[:, :, :], back).then_inc(s["bias_tile_loaded"], 16)

            def expert_load(m, q, expert):
                w, place = W_EXP[m]
                rows = D // NQ
                src = w[0][expert, q * rows:(q + 1) * rows, :].rearrange("a (k p) n -> p (a k) n", p=P)
                eng.dma_start(place[:, q * KC // NQ:(q + 1) * KC // NQ, :], src).then_inc(loaded[m][q], 16)

            first_late = STREAM.index(("gr", 0))
            for i in range(3, len(STREAM)):
                chunk(i)
                if first_late <= i < first_late + NQ:
                    expert_load("gate", i - first_late, slice(0, 1))
                    expert_load("up", i - first_late, slice(0, 1))
                if i == STREAM.index(("patt", 1)):
                    eng.wait_ge(s["rnn_ready"], 1)
                    eng.wait_ge(s["att_ready"], 4)
                    for q in range(NQ):
                        expert_load("gate_odd", q, slice(1, 2))
                if i == STREAM.index(("prnn", 1)):
                    eng.wait_ge(s["head_done"], H)
                    for t in range(TT):
                        eng.dma_start(x2[:, t, :], A["x"][0, t * P:(t + 1) * P, :]).then_inc(s["x_again_loaded"], 16)
            eng.wait_ge(s["bias_rows_cleared"], 1)
            eng.dma_start(brow[0:NE, 0, :], A["b_gate_e"][0]).then_inc(s["bias_rows_loaded"], 16)
            eng.dma_start(brow[0:NE, 1, :], A["b_up_e"][0]).then_inc(s["bias_rows_loaded"], 16)
            eng.wait_ge(s["unit_done"], unit("patt", 3) + 1)
            eng.dma_start(g2row, broadcast(A["norm_ffn_g"], D)).then_inc(s["ffn_norm_loaded"], 16)
            eng.wait_ge(s["down_biases_cleared"], 1)
            eng.dma_start(bdrow[0:NE, :], A["b_down_e"][0]).then_inc(s["bias_rows_loaded"], 16)
            eng.wait_ge(s["unit_done"], len(UNITS))
            for q in range(NQ):
                expert_load("down", q, slice(0, 1))
            eng.dma_start(gfrow, broadcast(A["norm_final_g"], D)).then_inc(s["final_norm_loaded"], 16)
            eng.wait_ge(s["job_table_ready"], 1)

            def expert_of(n):
                e = eng.value_load(jobi[0:1, n:n + 1] if isinstance(n, int) else jobi[0:1, bass.ds(n, 1)], min_val=0, max_val=NE - 1)
                return bass.ds(e, 1)

            def matrix(place, m, expert, n, extra=0):
                for q in range(NQ):
                    if m == "down" and q == NQ - 1:
                        eng.wait_ge(job["down_done"], n + (extra + 1))
                    else:
                        signals = NQ - 1 if m == "down" else NQ
                        eng.wait_ge(used[m], n * signals + (extra * signals + q + 1))
                    expert_load(place, q, expert)

            last4 = eng.value_load(jobi[0:1, JOBS + 2:JOBS + 3], min_val=NE - 4, max_val=JOBS - 6)
            matrix("gate", "gate", expert_of(2), 0)
            with eng.Fori(0, last4, 2) as j:
                first = expert_of(j + 1)
                matrix("up", "up", first, j)
                matrix("gate_odd", "gate", expert_of(j + 3), j, 1)
                matrix("down", "down", first, j)
                second = expert_of(j + 2)
                matrix("up", "up", second, j, 1)
                matrix("gate", "gate", expert_of(j + 4), j, 2)
                matrix("down", "down", second, j, 1)
            for n in range(3):
                expert = expert_of(last4 + (n + 1))
                matrix("up", "up", expert, last4, n)
                if n == 1:
                    matrix("gate_odd", "gate", expert_of(last4 + 3), last4, 1)
                matrix("down", "down", expert, last4, n)
            for t in range(TT):
                for half, ready in enumerate((s["fin_low"], s["fin_high"])):
                    eng.wait_ge(ready, t + 1)
                    eng.dma_start(out[0, t * P:(t + 1) * P, half * CH:(half + 1) * CH],
                                  h2[:, t, half * CH:(half + 1) * CH]).then_inc(s["out_stored"], 16)
            eng.wait_ge(s["out_stored"], 16 * 2 * TT)

        @block.gpsimd
        def _(eng):
            eng.memset(ident[:, :], 0.0).then_inc(s["identity_ready"], 1)
            eng.wait_ge(s["identity_ready"], 1)
            eng.affine_select(out=ident[:, :], in_=ident[:, :], compare_op=ALU.not_equal, fill=1.0, base=0,
                              pattern=[[-1, P]], channel_multiplier=1).then_inc(s["identity_ready"], 1)
            eng.wait_ge(s["identity_ready"], 2)
            eng.memset(rel[NBUCKET:NBUCKET + 1, :], NEG).then_inc(s["constants_ready"], 1)
            eng.wait_ge(s["constants_ready"], 1)
            eng.memset(blkd[:, :, :], 0.0).then_inc(s["block_diagonals_cleared"], 1)
            eng.wait_ge(s["block_diagonals_cleared"], 1)
            eng.memset(ones[:, :], 1.0).then_inc(s["constants_ready"], 1)
            eng.wait_ge(s["constants_ready"], 2)
            eng.iota(iota_slot[:, :].rearrange("p (a b) -> p a b", a=2), [[0, 2], [1, JB]], base=1,
                     channel_multiplier=0, allow_small_or_imprecise_dtypes=True).then_inc(s["constants_ready"], 1)
            eng.wait_ge(s["constants_ready"], 3)
            eng.iota(iota_job[:, :], [[1, JOBS]], base=0, channel_multiplier=0,
                     allow_small_or_imprecise_dtypes=True).then_inc(s["constants_ready"], 1)
            eng.wait_ge(s["constants_ready"], 4)
            eng.iota(ecol[:, :], [[1, 1]], base=0, channel_multiplier=1,
                     allow_small_or_imprecise_dtypes=True).then_inc(s["constants_ready"], 1)
            eng.wait_ge(s["constants_ready"], 5)
            eng.memset(tri[:, :], 1.0).then_inc(s["constants_ready"], 1)
            eng.wait_ge(s["constants_ready"], 6)
            eng.affine_select(out=tri[:, :], in_=tri[:, :], compare_op=ALU.is_ge, fill=0.0, base=0,
                              pattern=[[1, NE]], channel_multiplier=-1).then_inc(s["constants_ready"], 1)
            eng.wait_ge(s["constants_ready"], 7)
            eng.wait_ge(s["gates_done"], KC)
            eng.memset(qz[0][HD:P, :, :], 0.0).then_inc(s["query_zeros_ready"], 1)
            eng.wait_ge(s["query_zeros_ready"], 1)
            eng.memset(qz[1][0:HD, :, :], 0.0).then_inc(s["query_zeros_ready"], 1)
            eng.wait_ge(s["scores_ready"], H)
            eng.memset(gateT, 0.0).then_inc(s["gates_turned_cleared"], 1)
            eng.wait_ge(s["gates_turned_cleared"], 1)
            eng.wait_ge(s["unit_done"], unit("prnn", 3) + 1)
            eng.memset(brow[:, :, :], 0.0).then_inc(s["bias_rows_cleared"], 1)
            eng.wait_ge(s["bias_rows_cleared"], 1)
            eng.wait_ge(s["unit_done"], unit("patt", 3) + 1)
            eng.memset(bdrow, 0.0).then_inc(s["down_biases_cleared"], 1)
            eng.wait_ge(s["down_biases_cleared"], 1)
            eng.wait_ge(s["merged"], 4)
            eng.memset(ohj, 0.0).then_inc(s["job_tiles_cleared"], 1)

        @block.scalar
        def _(eng):
            for t in range(TT):
                eng.wait_ge(s[f"x_loaded_{t}"], 16)
                eng.activation(tile(2 + t)[:, 0:4, :].rearrange("p a b -> p (a b)"), hn[:, t, :], ACT.Square,
                               scale=D ** -0.5, accum_out=small[:, t, 0:1]).then_inc(s["x_squared"], 1)
                eng.wait_ge(s["x_ms"], t + 1)
                eng.activation(small[:, t, 3:4], small[:, t, 2:3], ACT.Sqrt).then_inc(s["x_std"], 1)
            eng.wait_ge(s["gain_ready"], 1)
            for t in range(TT):
                eng.wait_ge(s["norm_turned"], 2 * t + 1)
                for c in range(KC // 2):
                    eng.activation(hT[:, c, t * P:(t + 1) * P], bank[2 + 2 * t][:, c * P:(c + 1) * P],
                                   ACT.Copy, scale=gainT[:, c:c + 1]
                                   ).then_inc(s["norm_low_ready"], 1)
            eng.wait_ge(s["softplus_in"], 1)
            eng.activation(sp[:, 1, :], sp[:, 0, :], ACT.Exp, scale=-1.0).then_inc(s["softplus_exp"], 1)
            eng.wait_ge(s["lambda_sums_ready"], 2)
            eng.activation(lam[:, 2:4], lam[:, 0:2], ACT.Exp).then_inc(s["lambda_exps_ready"], 1)

            def unit_out(u):
                m, c, b = UNITS[u]
                ps = bank[u % 2]
                f = 4 * c + 2 * b
                eng.wait_ge(s["unit_done"], u + 1)
                if m == "v":
                    ins = eng.activation(vS[:, b, c * CH:(c + 1) * CH], ps[:, :], ACT.Copy)
                elif m == "q":
                    eng.wait_ge(s["query_zeros_ready"], 2)
                    eng.activation(qz[0][0:HD, f:f + 2, :], halves(ps)[0:HD], ACT.Copy, scale=HD ** -0.5)
                    ins = eng.activation(qz[1][HD:P, f:f + 2, :], halves(ps)[HD:P], ACT.Copy, scale=HD ** -0.5)
                elif m in ("g0", "g1"):
                    ins = eng.activation((iT if m == "g0" else rT)[:, f:f + 2, :], halves(ps), ACT.Tanh, scale=0.5)
                else:
                    if m == "gr":
                        eng.wait_ge(s["scan_ready"], 1)
                    ins = eng.activation({"xr": xrT, "k": kT, "gr": xrT}[m][:, f:f + 2, :], halves(ps), ACT.Copy)
                ins.then_inc(s["unit_out"], 1)

            for u in range(unit("xr"), unit("v", 3) + 1):
                unit_out(u)
            eng.wait_ge(s["vectors_ready"], 1)
            for n in range(KC):
                eng.wait_ge(s["gates_done"], n + 1)
                for b in range(2):
                    g, c = n // 4, 2 * (n % 4) + b
                    col = (V_BA, V_BX)[g] + c
                    ins = eng.activation((rT, iT)[g][:, c, :], bank[2 + n % 6][:, b * T:(b + 1) * T], ACT.Sigmoid,
                                         bias=pvT[:, col:col + 1])
                ins.then_inc(s["gates_out"], 1)
            for u in range(unit("q"), unit("q", 3) + 1):
                unit_out(u)
            eng.wait_ge(s["softplus_ready"], 1)
            eng.wait_ge(s["conv_ready"], 4)
            eng.wait_ge(s["gates_out"], KC)
            for c in range(KC):
                eng.activation(xrT[:, c, :], rT[:, c, :], ACT.Exp, scale=sp[:, 4, c:c + 1]
                               ).then_inc(s["decay_ready"], 1)
            unit_out(unit("k"))
            eng.wait_ge(s["bias_tile_loaded"], 16)
            for c in range(KC):
                eng.activation(yrT[:, c, :], rT[:, c, :], ACT.Tanh, scale=sp[:, 5, c:c + 1]
                               ).then_inc(s["decay_ready"], 1)
            for n in range(1, 4):
                unit_out(unit("k", n))
            eng.wait_ge(s["multiplier_in"], 1)
            eng.activation(rT[:, :, :], rT[:, :, :], ACT.Sqrt).then_inc(s["multiplier_ready"], 1)

            def exps(h):
                b = h % 2
                eng.wait_ge(s["scores_ready"], h + 1)
                for n, (o, w) in enumerate(((0, 256), (256, 256), (512, 128), (640, 128))):
                    eng.activation(sc[:, b, o:o + w], sc[:, b, o:o + w], ACT.Exp, bias=st[:, b, n:n + 1],
                                   accum_out=st[:, b, 4 + n:5 + n]).then_inc(s["exps_done"], 1)

            def weights_out(h):
                if h >= 1:
                    eng.wait_ge(s["head_done"], h)
                eng.wait_ge(s["weights_turned"], h + 1)
                eng.activation(wT[:, :], bank[5][:, 0:384], ACT.Copy).then_inc(s["weights_out"], 1)

            def head_out(h):
                eng.wait_ge(s["head_done"], h + 1)
                eng.activation(oT[:, h, :], bank[6][:, 0:T], ACT.Copy
                               ).then_inc(s["head_out"], 1)

            for step in range(12):
                unit_out(unit("gr") + step)
                if step < H:
                    exps(step)
                if 1 <= step <= H:
                    weights_out(step - 1)
                if 2 <= step <= H + 1:
                    head_out(step - 2)
                if step == 4:
                    eng.wait_ge(s["unit_out"], unit("gr", 3) + 1)
                    eng.activation(xcT[:, :, :], xrT[:, :, :], ACT.Square).then_inc(s["gelu_square"], 1)
                if step == 7:
                    eng.wait_ge(s["gelu_in"], 1)
                    eng.activation(xcT[:, :, :], xcT[:, :, :], ACT.Tanh, scale=GELU_B).then_inc(s["gelu_tanh"], 1)
            eng.wait_ge(s["head_out"], H)
            eng.activation(osq[:, :, :], oT[:, :, :], ACT.Square).then_inc(s["heads_squared"], 1)
            eng.wait_ge(s["heads_ms"], 4)
            eng.activation(orr[:, :, :], orr[:, :, :], ACT.Sqrt).then_inc(s["heads_std"], 1)

            def squares(ready, squared, first):
                for n in range(first, first + 2):
                    t, c = divmod(n, 2)
                    eng.wait_ge(ready, n + 1)
                    if n > 0:
                        eng.wait_ge(squared, n)
                    eng.activation(junk, x2[:, t, c * CH:(c + 1) * CH], ACT.Square, scale=D ** -0.5,
                                   accum_out=small[:, t, c:c + 1]).then_inc(squared, 1)

            def norm(t, name, done):
                eng.wait_ge(s[f"{name}_ms"], t + 1)
                eng.activation(small[:, t, 3:4], small[:, t, 2:3], ACT.Sqrt).then_inc(s[f"{name}_std"], 1)
                eng.wait_ge(s[f"{name}_gained"], t + 1)
                eng.wait_ge(s[f"{name}_inverse"], t + 1)
                eng.activation(h2[:, t, CH:D], h2[:, t, CH:D], ACT.Copy, scale=small[:, t, 4:5]).then_inc(done, 1)

            def exps_of_logits(t):
                eng.wait_ge(s["top_ready"], t + 1)
                eng.activation(r_exp[:, t, :], r_log[:, t, :], ACT.Exp, bias=r_nmx[:, t:t + 1]
                               ).then_inc(s["route_exps"], 1)

            eng.wait_ge(s["merged"], 4)
            for t in range(TT):
                squares(s["mixed"], s["mixed_squared"], 2 * t)
                norm(t, "mixed", s["ffn_high"])
                if t == 1:
                    eng.activation(st[:, 0, 0:1], ones[:, 0:1], ACT.Exp)
                eng.wait_ge(s["ffn_turned"], 2 * t + 1)
                eng.activation(hfT[:, 0:4, t * P:(t + 1) * P], quarters(bank[2 + 2 * t]), ACT.Copy
                               ).then_inc(s["ffn_low_out"], 1)
            for t in range(TT):
                exps_of_logits(t)
            eng.activation(st[:, 0, 0:1], ones[:, 0:1], ACT.Sigmoid)
            eng.wait_ge(s["gates_turned_cleared"], 1)
            eng.wait_ge(s["weight_turned"], 1)
            eng.activation(gateT[0:NE, :], bank[1][0:NE, 0:T], ACT.Copy).then_inc(s["weight_out"], 1)

            eng.sem_inc(job["activation_out"], 1)
            eng.sem_inc(job["output_out"], 1)
            eng.wait_ge(job["gathered"], 1)
            eng.activation(xg, bank[2][:, :], ACT.Copy).then_inc(job["gather_out"], 1)
            eng.wait_ge(job["gather_turned"], 1)
            eng.activation(xgT[0], quarters(bank[2]), ACT.Copy).then_inc(job["input"], 1)
            eng.wait_ge(s["job_table_ready"], 1)
            jobs = eng.value_load(jobi[0:1, JOBS:JOBS + 1], min_val=NE, max_val=JOBS - 2)

            def one_job(j, parity):
                eng.wait_ge(job["activation"], j + 1)
                eng.wait_ge(job["gate_clamped"], j + 1)
                eng.activation(sg, gm, ACT.Sigmoid, scale=SWIGLU_ALPHA).then_inc(job["sigmoid"], 1)
                eng.wait_ge(job["gathered"], j + 2)
                eng.activation(xg, bank[2][:, :], ACT.Copy).then_inc(job["gather_out"], 1)
                eng.wait_ge(job["gather_turned"], j + 2)
                eng.activation(xgT[1 - parity], quarters(bank[2]), ACT.Copy).then_inc(job["input"], 1)
                if parity == 0:
                    eng.wait_ge(job["scattered"], j + 1)
                eng.wait_ge(job["scatter_turned"], j + 2)
                turned = bank[3][:, 0:TT * P].rearrange("p (t n) -> p t n", t=TT)
                eng.activation(scat[0:JB, parity], turned[0:JB], ACT.Copy)
                eng.activation(scat[JB:P, 1 - parity], turned[JB:P], ACT.Copy).then_inc(job["scatter_ready"], 1)
                eng.wait_ge(job["activation_turned"], j + 2)
                eng.activation(avT, quarters(bank[1]), ACT.Copy).then_inc(job["activation_out"], 1)
                eng.wait_ge(job["down_done"], j + 1)
                eng.activation(ys[1 - parity][JB:P], bank[3][JB:P, :], ACT.Copy).then_inc(job["output_half_out"], 1)
                eng.activation(ys[parity][0:JB], bank[3][0:JB, :], ACT.Copy).then_inc(job["output_out"], 1)

            with eng.Fori(0, jobs, 2) as j:
                one_job(j, 0)
                one_job(j + 1, 1)
            eng.activation(st[:, 0, 0:1], ones[:, 0:1], ACT.Sqrt)
            for t in range(TT):
                squares(s["result_ready"], s["result_squared"], 2 * t)
                norm(t, "result", s["fin_high"])

        @block.vector
        def _(eng):
            count = [0]

            def link(ins):
                count[0] += 1
                ins.then_inc(dve_order, 1)
                eng.wait_ge(dve_order, count[0])

            for t in range(TT):
                eng.wait_ge(s["x_squared"], t + 1)
                eng.tensor_scalar(small[:, t, 2:3], small[:, t, 0:1], EPS, None, ALU.add).then_inc(s["x_ms"], 1)
                eng.wait_ge(s["x_std"], t + 1)
                link(eng.reciprocal(small[:, t, 4:5], small[:, t, 3:4]))
                eng.tensor_scalar(hn[:, t, :], hn[:, t, :], small[:, t, 4:5], None, ALU.mult
                                  ).then_inc(s["x_normed"], 1)
                if t == 0:
                    eng.wait_ge(s["gain_turned"], 1)
                    eng.tensor_copy(gainT[:, :], bank[7][:, 0:KC]).then_inc(s["gain_ready"], 1)
            eng.wait_ge(s["gain_ready"], 1)
            for t in range(TT):
                eng.wait_ge(s["norm_turned"], 2 * t + 2)
                for c in range(KC // 2, KC):
                    eng.tensor_scalar(hT[:, c, t * P:(t + 1) * P], bank[3 + 2 * t][:, (c - 4) * P:(c - 3) * P],
                                      gainT[:, c:c + 1], None, ALU.mult
                                      ).then_inc(s["norm_high_ready"], 1)
            eng.wait_ge(s["vectors_turned"], 1)
            eng.tensor_copy(pvT[:, :], bank[7][:, 0:NV]).then_inc(s["vectors_ready"], 1)
            eng.wait_ge(s["bias_vector_done"], 1)
            eng.tensor_copy(bias_vec, bank[6][0:H, 0:DIFFS]).then_inc(s["bias_vector_ready"], 1)
            eng.wait_ge(s["vectors_ready"], 1)
            lruT = pvT[:, V_LAM:V_LAM + KC]
            eng.scalar_tensor_tensor(out=sp[:, 0, :], in0=lruT, scalar=-1.0, in1=lruT, op0=ALU.mult,
                                     op1=ALU.max).then_inc(s["softplus_in"], 1)
            link(eng.tensor_scalar(sp[:, 6, :], lruT, -1.0, 0.0, ALU.mult, ALU.max))
            eng.wait_ge(s["softplus_exp"], 1)
            link(eng.tensor_scalar(sp[:, 2, :], sp[:, 1, :], 2.0, None, ALU.add))
            link(eng.reciprocal(sp[:, 3, :], sp[:, 2, :]))
            link(eng.tensor_tensor(sp[:, 2, :], sp[:, 1, :], sp[:, 3, :], ALU.mult))
            link(eng.tensor_tensor(sp[:, 3, :], sp[:, 2, :], sp[:, 2, :], ALU.mult))
            link(eng.tensor_scalar(sp[:, 7, :], sp[:, 3, :], 1.0 / 19, None, ALU.mult))
            for k in range(8, 0, -1):
                link(eng.scalar_tensor_tensor(out=sp[:, 7, :], in0=sp[:, 7, :], scalar=1.0 / (2 * k + 1),
                                              in1=sp[:, 3, :], op0=ALU.add, op1=ALU.mult))
            link(eng.scalar_tensor_tensor(out=sp[:, 7, :], in0=sp[:, 7, :], scalar=1.0, in1=sp[:, 2, :],
                                          op0=ALU.add, op1=ALU.mult))
            link(eng.scalar_tensor_tensor(out=sp[:, 7, :], in0=sp[:, 7, :], scalar=2.0, in1=sp[:, 6, :],
                                          op0=ALU.mult, op1=ALU.add))
            link(eng.tensor_scalar(sp[:, 4, :], sp[:, 7, :], -RGLRU_C, None, ALU.mult))
            eng.tensor_scalar(sp[:, 5, :], sp[:, 7, :], RGLRU_C, None, ALU.mult).then_inc(s["softplus_ready"], 1)
            eng.wait_ge(s["lambda_vectors_loaded"], 64)
            for n in range(2):
                link(eng.tensor_tensor(lamv[:, 2 * n, :], lamv[:, 2 * n, :], lamv[:, 2 * n + 1, :], ALU.mult))
                eng.reduce_sum(lam[:, n:n + 1], lamv[:, 2 * n, :], AX_X).then_inc(s["lambda_sums_ready"], 1)
            eng.wait_ge(s["lambda_exps_ready"], 1)
            link(eng.tensor_tensor(lam[:, 4:5], lam[:, 3:4], lam[:, 2:3], ALU.subtract))
            link(eng.tensor_scalar(lam[:, 5:6], lam[:, 4:5], -LAM_INIT, None, ALU.add))
            link(eng.tensor_scalar(lam[:, 6:7], pvT[:, V_SUB:V_SUB + 1], 1.0 - LAM_INIT, None, ALU.mult))

            for n in range(4):
                eng.wait_ge(s["unit_out"], n + 1)
                for c in (2 * n, 2 * n + 1):
                    def tap(w):
                        return pvT[:, V_CONVW + w * KC + c:V_CONVW + w * KC + c + 1]
                    link(eng.tensor_scalar(xcT[:, c, :], xrT[:, c, :], tap(3), pvT[:, V_CONVB + c:V_CONVB + c + 1],
                                           ALU.mult, ALU.add))
                    for back in (1, 2, 3):
                        ins = eng.scalar_tensor_tensor(out=xcT[:, c, back:], in0=xrT[:, c, 0:T - back],
                                                       scalar=tap(3 - back), in1=xcT[:, c, back:],
                                                       op0=ALU.mult, op1=ALU.add)
                        if back < 3 or c % 2 == 0:
                            link(ins)
                ins.then_inc(s["conv_ready"], 1)
            eng.wait_ge(s["conv_ready"], 4)
            eng.wait_ge(s["gates_out"], KC)
            eng.wait_ge(s["gates_done"], KC)
            link(eng.tensor_tensor(iT[:, :, :], iT[:, :, :], xcT[:, :, :], ALU.mult))
            eng.wait_ge(s["decay_ready"], 2 * KC)
            link(eng.tensor_scalar(xcT[:, :, :], yrT[:, :, :], 1.0, None, ALU.add))
            link(eng.reciprocal(xcT[:, :, :], xcT[:, :, :]))
            eng.scalar_tensor_tensor(out=rT[:, :, :], in0=yrT[:, :, :], scalar=2.0, in1=xcT[:, :, :],
                                     op0=ALU.mult, op1=ALU.mult).then_inc(s["multiplier_in"], 1)
            eng.wait_ge(s["multiplier_ready"], 1)
            link(eng.tensor_tensor(iT[:, :, :], iT[:, :, :], rT[:, :, :], ALU.mult))
            for c in range(KC):
                ins = eng.tensor_tensor_scan(yrT[:, c, :], xrT[:, c, :], iT[:, c, :], 0.0, ALU.mult, ALU.add)
            ins.then_inc(s["scan_ready"], 1)

            def scores_in(h):
                b = h % 2
                eng.wait_ge(s["scores_done"], h + 1)
                s1 = sc[:, b, 0:512].rearrange("p (n k) -> p n k", n=2)
                s0 = sc[:, b, 512:768].rearrange("p (n k) -> p n k", n=2)
                ps0 = bank[4][:, 0:T].rearrange("p (n k) -> p n k", n=2)
                if h == 0:
                    eng.wait_ge(s["bias_tile_loaded"], 16)
                link(eng.tensor_tensor(s1, halves(bank[2 + b]), tb[:, h:h + 1, :].to_broadcast([P, 2, T]), ALU.add))
                link(eng.tensor_tensor(s0, ps0, tb[:, h:h + 1, P:T].to_broadcast([P, 2, P]), ALU.add))
                eng.tensor_reduce(st[:, b, 8:10], s1, AX_X, ALU.max)
                link(eng.tensor_reduce(st[:, b, 10:12], s0, AX_X, ALU.max))
                eng.tensor_scalar(st[:, b, 0:4], st[:, b, 8:12], -1.0, None, ALU.mult
                                  ).then_inc(s["scores_ready"], 1)

            def weights_in(h):
                b = h % 2
                eng.wait_ge(s["exps_done"], 4 * (h + 1))
                link(eng.reciprocal(st[:, b, 8:12], st[:, b, 4:8]))
                link(eng.tensor_scalar(st[:, b, 4:8], st[:, b, 8:12], lam[:, 5:6], None, ALU.mult))
                eng.tensor_scalar(sc[:, b, 256:512], sc[:, b, 256:512], st[:, b, 5:6], None, ALU.mult)
                link(eng.tensor_scalar(sc[:, b, 640:768], sc[:, b, 640:768], st[:, b, 7:8], None, ALU.mult))
                if h >= 1:
                    eng.wait_ge(s["weights_turned"], h)
                eng.scalar_tensor_tensor(out=wm[:, 0:256], in0=sc[:, b, 0:256], scalar=st[:, b, 8:9],
                                         in1=sc[:, b, 256:512], op0=ALU.mult, op1=ALU.add)
                eng.scalar_tensor_tensor(out=wm[:, 256:384], in0=sc[:, b, 512:640], scalar=st[:, b, 10:11],
                                         in1=sc[:, b, 640:768], op0=ALU.mult, op1=ALU.add
                                         ).then_inc(s["weights_ready"], 1)

            for step in range(12):
                if 1 <= step <= H:
                    weights_in(step - 1)
                if step < H:
                    scores_in(step)
                if step == 5:
                    eng.wait_ge(s["gelu_square"], 1)
                    link(eng.tensor_scalar(xcT[:, :, :], xcT[:, :, :], GELU_A, 1.0, ALU.mult, ALU.add))
                    eng.tensor_tensor(xcT[:, :, :], xcT[:, :, :], xrT[:, :, :], ALU.mult).then_inc(s["gelu_in"], 1)
                if step == 9:
                    eng.wait_ge(s["gelu_tanh"], 1)
                    link(eng.scalar_tensor_tensor(out=xcT[:, :, :], in0=xcT[:, :, :], scalar=1.0, in1=xrT[:, :, :],
                                                  op0=ALU.add, op1=ALU.mult))
                    eng.wait_ge(s["scan_ready"], 1)
                    eng.scalar_tensor_tensor(out=yrT[:, :, :], in0=xcT[:, :, :], scalar=0.5, in1=yrT[:, :, :],
                                             op0=ALU.mult, op1=ALU.mult).then_inc(s["rnn_ready"], 1)

            def gated(u):
                m, c, b = UNITS[u]
                f = 4 * c + 2 * b
                g = iT if m == "prnn" else rT
                eng.wait_ge(s["unit_done"], u + 1)
                ins = eng.scalar_tensor_tensor(out=g[:, f:f + 2, :], in0=g[:, f:f + 2, :], scalar=1.0,
                                               in1=halves(bank[u % 2]), op0=ALU.add, op1=ALU.mult)
                ins.then_inc(s["projection_out"], 1)
                if m == "patt":
                    eng.wait_ge(s["projection_out"], u + 1 - unit("prnn"))
                    eng.tensor_tensor(iT[:, f:f + 2, :], iT[:, f:f + 2, :], rT[:, f:f + 2, :], ALU.add
                                      ).then_inc(s["merged"], 1)

            eng.wait_ge(s["unit_out"], unit("g1", 3) + 1)
            gated(unit("prnn"))
            eng.wait_ge(s["heads_summed"], 4)
            for n in range(4):
                eng.tensor_scalar(orr[:, 2 * n:2 * n + 2, :], halves(bank[2 + n]), 1.0 / VD, EPS, ALU.mult, ALU.add
                                  ).then_inc(s["heads_ms"], 1)
            gated(unit("prnn", 1))
            eng.wait_ge(s["heads_std"], 1)
            for n in range(4):
                two = slice(2 * n, 2 * n + 2)
                link(eng.reciprocal(orr[:, two, :], orr[:, two, :]))
                eng.scalar_tensor_tensor(out=yaT[:, two, :], in0=oT[:, two, :], scalar=lam[:, 6:7], in1=orr[:, two, :],
                                         op0=ALU.mult, op1=ALU.mult).then_inc(s["att_ready"], 1)
                if n == 1:
                    gated(unit("prnn", 2))
            for u in range(unit("prnn", 3), unit("patt", 3) + 1):
                gated(u)
            eng.wait_ge(s["x_again_loaded"], 16 * TT)
            def norm(t, name, gain, done):
                eng.tensor_tensor(h2[:, t, :], x2[:, t, :], gain, ALU.mult).then_inc(s[f"{name}_gained"], 1)
                eng.wait_ge(s[f"{name}_squared"], 2 * t + 2)
                eng.tensor_scalar(small[:, t, 2:3], small[:, t, 0:1], small[:, t, 1:2], EPS, ALU.add, ALU.add
                                  ).then_inc(s[f"{name}_ms"], 1)
                eng.wait_ge(s[f"{name}_std"], t + 1)
                eng.reciprocal(small[:, t, 4:5], small[:, t, 3:4]).then_inc(s[f"{name}_inverse"], 1)
                eng.wait_ge(s[f"{name}_inverse"], t + 1)
                eng.wait_ge(s[f"{name}_gained"], t + 1)
                eng.tensor_scalar(h2[:, t, 0:CH], h2[:, t, 0:CH], small[:, t, 4:5], None, ALU.mult).then_inc(done, 1)

            for t in range(TT):
                for c in range(2):
                    u = unit("out", 2 * t + c)
                    eng.wait_ge(s["unit_done"], u + 1)
                    part = x2[:, t, c * CH:(c + 1) * CH]
                    eng.scalar_tensor_tensor(out=part, in0=bank[u % 2][:, :], scalar=0.5, in1=part, op0=ALU.mult,
                                             op1=ALU.add).then_inc(s["mixed"], 1)
                    if (t, c) == (1, 0):
                        eng.wait_ge(s["ffn_turned"], 2)
                        eng.tensor_copy(hfT[:, 4:8, 0:P], quarters(bank[3])).then_inc(s["ffn_high_out"], 1)
                if t == 0:
                    eng.wait_ge(s["ffn_norm_loaded"], 16)
                eng.wait_ge(s["mixed"], 2 * t + 2)
                norm(t, "mixed", g2row, s["ffn_low"])

            def top(t):
                eng.wait_ge(s["logits_done"], t + 1)
                link(eng.tensor_copy(r_log[:, t, :], bank[2 + t][:, 0:NE]))
                link(eng.max(r_max[:, t, :], r_log[:, t, :]))
                eng.tensor_scalar(r_nmx[:, t:t + 1], r_max[:, t, 0:1], -1.0, None, ALU.mult
                                  ).then_inc(s["top_ready"], 1)

            def choose(t):
                fourth = r_max[:, t, TOPK - 1:TOPK]
                eng.tensor_scalar(r_eq[:, t, :], r_log[:, t, :], fourth, None, ALU.is_equal)
                link(eng.tensor_scalar(r_gt[:, t, :], r_log[:, t, :], fourth, None, ALU.is_gt))
                eng.tensor_tensor_scan(r_rank[:, t, :], ones[:, 0:NE], r_eq[:, t, :], 0.0, ALU.mult, ALU.add)
                link(eng.tensor_reduce(r_ngt[:, t:t + 1], r_gt[:, t, :], AX_X, ALU.add))
                link(eng.tensor_scalar(r_need[:, t:t + 1], r_ngt[:, t:t + 1], -1.0, float(TOPK), ALU.mult, ALU.add))
                link(eng.scalar_tensor_tensor(out=r_rank[:, t, :], in0=r_rank[:, t, :], scalar=r_need[:, t:t + 1],
                                              in1=r_eq[:, t, :], op0=ALU.is_le, op1=ALU.mult))
                eng.tensor_tensor(r_mask[:, t, :], r_gt[:, t, :], r_rank[:, t, :], ALU.add
                                  ).then_inc(s["mask_ready"], 1)
                eng.wait_ge(s["mask_ready"], t + 1)
                eng.wait_ge(s["route_exps"], t + 1)
                link(eng.tensor_tensor(r_exp[:, t, :], r_exp[:, t, :], r_mask[:, t, :], ALU.mult))
                link(eng.tensor_reduce(r_sum[:, t:t + 1], r_exp[:, t, :], AX_X, ALU.add))
                link(eng.reciprocal(r_inv[:, t:t + 1], r_sum[:, t:t + 1]))
                eng.tensor_scalar(r_gate[:, t, :], r_exp[:, t, :], r_inv[:, t:t + 1], None, ALU.mult
                                  ).then_inc(s["weight_ready"], 1)

            def logits_in(t):
                eng.wait_ge(s["logits_turned"], t + 1)
                eng.tensor_scalar(r_logT[:, t * P:(t + 1) * P], bank[6 + t][0:NE, 0:P], brt[:, 0:1], None, ALU.add
                                  ).then_inc(s["logits_biased"], 1)

            eng.wait_ge(s["router_loaded"], 32)
            logits_in(0)
            top(0)
            eng.wait_ge(s["ffn_turned"], 4)
            eng.tensor_copy(hfT[:, 4:8, P:T], quarters(bank[5])).then_inc(s["ffn_high_out"], 1)
            choose(0)
            logits_in(1)
            top(1)
            choose(1)
            eng.wait_ge(s["mask_turned"], 1)
            maskT = bank[0][0:NE, 0:T]
            link(eng.tensor_tensor_scan(inclT, ones[0:NE, 0:T], maskT, 0.0, ALU.mult, ALU.add))
            eng.tensor_tensor(slotT, inclT, maskT, ALU.mult).then_inc(s["slots_ready"], 1)
            total = inclT[:, T - 1:T]
            link(eng.tensor_scalar(novf, total, float(JB), None, ALU.is_gt))
            for b in range(2, T // JB):
                ins = eng.scalar_tensor_tensor(out=novf, in0=total, scalar=float(b * JB), in1=novf, op0=ALU.is_gt,
                                               op1=ALU.add)
                if b < T // JB - 1:
                    link(ins)
            ins.then_inc(s["overflow_ready"], 1)
            eng.wait_ge(s["slot_columns_done"], 1)
            eng.wait_ge(s["job_tiles_cleared"], 1)
            eng.tensor_copy(jcol[:, :, 0:NE], bank[0][:, 0:TT * NE].rearrange("p (t e) -> p t e", t=TT)
                            ).then_inc(s["slot_columns_ready"], 1)

            def select(n):
                for t in range(TT):
                    ins = eng.tensor_scalar(sel[:, t, :], iota_slot[:, 0:JB], jcol[:, t, n], None, ALU.is_equal)
                ins.then_inc(job["selection"], 1)

            def expert_onehot(n):
                eng.tensor_scalar(ohb, ones[:, 0:JB], ohj[:, n], None, ALU.mult).then_inc(job["expert_onehot"], 1)

            eng.wait_ge(s["slot_columns_ready"], 1)
            select(slice(0, 1))
            eng.wait_ge(s["ends_done"], 1)
            eng.tensor_copy(extra, bank[3][0:1, 1:2])
            link(eng.tensor_copy(ends, bank[3][0:NE, 0:1]))
            link(eng.tensor_tensor(starts, ends, novf, ALU.subtract))
            more = iota_job[:, 0:MORE]
            eng.tensor_copy(ohj[0:NE, 0:NE], ident[0:NE, 0:NE])
            link(eng.tensor_scalar(owork, more, ends, None, ALU.is_lt))
            link(eng.scalar_tensor_tensor(out=ohj[0:NE, NE:JOBS], in0=more, scalar=starts, in1=owork, op0=ALU.is_ge,
                                          op1=ALU.mult))
            link(eng.tensor_scalar(owork, more, starts, -float(JB), ALU.subtract, ALU.mult))
            eng.scalar_tensor_tensor(out=block64, in0=owork, scalar=-float(JB), in1=ohj[0:NE, NE:JOBS],
                                     op0=ALU.add, op1=ALU.mult).then_inc(s["jobs_ready"], 1)
            eng.sem_inc(job["activation"], 1)
            eng.sem_inc(job["up_clamped"], 1)
            expert_onehot(slice(0, 1))
            evens = iota_job[0:1, 0:MORE].rearrange("p (a b) -> p a b", b=2)[:, :, 0]
            link(eng.tensor_scalar(under, evens, extra, None, ALU.is_lt))
            link(eng.tensor_reduce(pairs, under, AX_X, ALU.add))
            for n in range(3):
                eng.tensor_scalar(jobi[0:1, JOBS + n:JOBS + n + 1], pairs, 2.0, float(NE - 2 * n), ALU.mult, ALU.add)
            eng.wait_ge(s["late_columns_done"], 1)
            late = bank[3][:, 0:TT * MORE].rearrange("p (t n) -> p t n", t=TT)
            eng.tensor_copy(jcol[:, :, NE:JOBS], late)
            eng.tensor_copy(gcol, bank[3][:, TT * MORE:TT * (MORE + JOBS)].rearrange("p (t n) -> p t n", t=TT))
            eng.tensor_copy(jobi[0:1, 0:JOBS], bank[3][0:1, 256:256 + JOBS]).then_inc(s["job_table_ready"], 1)
            eng.wait_ge(s["job_table_ready"], 1)
            jobs = eng.value_load(jobi[0:1, JOBS:JOBS + 1], min_val=NE, max_val=JOBS - 2)
            with eng.Fori(0, jobs) as j:
                eng.wait_ge(job["gathered"], j + 1)
                select(bass.ds(j + 1, 1))
                eng.wait_ge(job["scatter_turned"], j + 1)
                for t in range(TT):
                    ins = eng.tensor_scalar(selw[:, t, :], iota_slot[:, :], jcol[:, t, bass.ds(j, 1)],
                                            gcol[:, t, bass.ds(j, 1)], ALU.is_equal, ALU.mult)
                ins.then_inc(job["weighted_selection"], 1)
                eng.wait_ge(job["gate_done"], j + 1)
                eng.tensor_scalar(gm, bank[0][:, :], LIMIT, None, ALU.min).then_inc(job["gate_clamped"], 1)
                eng.wait_ge(job["gate_clamped"], j + 1)
                eng.wait_ge(job["sigmoid"], j + 1)
                eng.tensor_tensor(gm, gm, sg, ALU.mult).then_inc(job["gate_ready"], 1)
                eng.wait_ge(job["up_done"], j + 1)
                eng.tensor_scalar(uc, bank[1][:, :], LIMIT, -LIMIT, ALU.min, ALU.max).then_inc(job["up_clamped"], 1)
                eng.wait_ge(job["gate_ready"], j + 1)
                eng.wait_ge(job["up_clamped"], j + 2)
                eng.wait_ge(job["activation_turned"], j + 1)
                eng.scalar_tensor_tensor(out=av, in0=uc, scalar=1.0, in1=gm, op0=ALU.add, op1=ALU.mult
                                         ).then_inc(job["activation"], 1)
                expert_onehot(bass.ds(j + 1, 1))
            eng.wait_ge(s["final_norm_loaded"], 16)
            for t in range(TT):
                for h in range(2):
                    eng.wait_ge(job["scattered_first"] if t == 0 else job["scattered"], jobs + h)
                    part = x2[:, t, h * CH:(h + 1) * CH]
                    eng.tensor_tensor(part, bank[4 + 2 * t + h][:, :], part, ALU.add).then_inc(s["result_ready"], 1)
                eng.wait_ge(s["result_ready"], 2 * t + 2)
                norm(t, "result", gfrow, s["fin_low"])

        @block.tensor
        def _(eng):
            eng.wait_ge(s["identity_ready"], 2)
            eng.wait_ge(s["gain_loaded"], 16)
            eng.transpose(bank[7][:, 0:KC], gain[:, :], ident[0:KC, 0:KC]).then_inc(s["gain_turned"], 1)
            def turn(src, t, ready, turned):
                for half in range(2):
                    eng.wait_ge(ready[half], t + 1)
                    for c in range(4):
                        f = 4 * half + c
                        ins = eng.transpose(bank[2 + 2 * t + half][:, c * P:(c + 1) * P], src[:, t, f * P:(f + 1) * P],
                                            ident[:, :])
                    ins.then_inc(turned, 1)

            for t in range(TT):
                turn(hn, t, [s["x_normed"]] * 2, s["norm_turned"])

            def product(u, rhs=None, lhsT=None, ready=None):
                m, c, b = UNITS[u]
                i = STREAM.index((m, c))
                if b == 0:
                    eng.wait_ge(chunk_loaded[i % 2], 16 * (i // 2 + 1))
                if u >= 2:
                    if u - 2 < unit("prnn"):
                        eng.wait_ge(s["unit_out"], u - 1)
                    elif u - 2 < unit("out"):
                        eng.wait_ge(s["projection_out"], u - 1 - unit("prnn"))
                    else:
                        eng.wait_ge(s["mixed"], u - 1 - unit("out"))
                w = wst[:, i % 2]
                ps = bank[u % 2]
                if rhs is not None:
                    for n in range(2):
                        for k in range(KC):
                            if ready is not None and n == 0:
                                eng.wait_ge(*ready(k))
                            ins = eng.matmul(ps[:, n * T:(n + 1) * T], w[:, k, (2 * b + n) * P:(2 * b + n + 1) * P],
                                             rhs[:, k, :], start=(k == 0), stop=(k == KC - 1))
                else:
                    for k in range(KC):
                        if ready is not None:
                            eng.wait_ge(*ready(k))
                        ins = eng.matmul(ps[:, :], lhsT[:, k, b * P:(b + 1) * P], w[:, k, :],
                                         start=(k == 0), stop=(k == KC - 1))
                ins.then_inc(s["unit_done"], 1)

            for n in range(4):
                product(unit("xr") + n, rhs=hT, ready=None if n else lambda k: (
                    (s["norm_low_ready"], KC // 2 + k + 1) if k < KC // 2 else (s["norm_high_ready"], k + 1)))
                if n == 0:
                    eng.wait_ge(s["gain_ready"], 1)
                    eng.wait_ge(s["vectors_loaded"], 16 * 6)
                    eng.transpose(bank[7][:, 0:NV], pv[:, :], ident[0:NV, 0:NV]).then_inc(s["vectors_turned"], 1)
                    eng.wait_ge(s["constants_ready"], 1)
                    eng.wait_ge(s["rel_loaded"], 16)
                    eng.wait_ge(s["onehot_loaded"], 16)
                    eng.matmul(bank[6][0:H, 0:DIFFS], rel[:, :], onehot, start=True, stop=True
                               ).then_inc(s["bias_vector_done"], 1)
            for n in range(4):
                product(unit("v") + n, lhsT=hT)
            eng.wait_ge(s["block_diagonals_loaded"], 64)
            for n in range(KC):
                eng.wait_ge(s["conv_ready"], min(n, 3) + 1)
                if n >= 6:
                    eng.wait_ge(s["gates_out"], n - 5)
                for b in range(2):
                    g, c = n // 4, 2 * (n % 4) + b
                    ins = eng.matmul(bank[2 + n % 6][:, b * T:(b + 1) * T], blkd[:, g * KC + c, :], xcT[:, c, :],
                                     start=True, stop=True)
                ins.then_inc(s["gates_done"], 1)
            for n in range(4):
                product(unit("q") + n, rhs=hT)
            for n in range(4):
                product(unit("k") + n, rhs=hT)
            eng.wait_ge(s["gates_out"], KC)

            def scores(h):
                if h == 0:
                    eng.wait_ge(s["unit_out"], unit("k", 3) + 1)
                if h >= 1:
                    eng.wait_ge(s["scores_ready"], h)
                for n in range(2):
                    eng.matmul(bank[2 + h % 2][:, n * T:(n + 1) * T], qz[n][:, h, P:T], kT[:, h, :],
                               start=True, stop=True)
                for n in range(2):
                    ins = eng.matmul(bank[4][:, n * P:(n + 1) * P], qz[n][:, h, 0:P], kT[:, h, 0:P], start=True, stop=True)
                ins.then_inc(s["scores_done"], 1)

            def turn_weights(h):
                eng.wait_ge(s["weights_ready"], h + 1)
                if h >= 1:
                    eng.wait_ge(s["weights_out"], h)
                eng.transpose(bank[5][:, 0:P], wm[:, 256:384], ident[:, :])
                eng.transpose(bank[5][:, P:2 * P], wm[:, 0:P], ident[:, :])
                eng.transpose(bank[5][:, 2 * P:3 * P], wm[:, P:2 * P], ident[:, :]).then_inc(s["weights_turned"], 1)

            def head(h):
                eng.wait_ge(s["weights_out"], h + 1)
                if h >= 1:
                    eng.wait_ge(s["head_out"], h)
                v = [vS[:, t, h * VD:(h + 1) * VD] for t in range(TT)]
                eng.matmul(bank[6][:, 0:P], v[0], wT[:, 0:P], start=True, stop=True)
                eng.matmul(bank[6][:, P:T], v[0], wT[:, P:T], start=True, stop=False)
                eng.matmul(bank[6][:, P:T], v[1], wT[:, T:T + P], start=False, stop=True
                           ).then_inc(s["head_done"], 1)

            for step in range(12):
                product(unit("gr") + step, rhs=hT)
                if step < H:
                    scores(step)
                if 1 <= step <= H:
                    turn_weights(step - 1)
                if 2 <= step <= H + 1:
                    head(step - 2)
            eng.wait_ge(s["rnn_ready"], 1)
            product(unit("prnn"), rhs=yrT)
            eng.wait_ge(s["heads_squared"], 1)
            for n in range(4):
                eng.matmul(bank[2 + n][:, :], ones[:, 0:P], osq[:, 2 * n:2 * n + 2, :].rearrange("p a b -> p (a b)"),
                           start=True, stop=True).then_inc(s["heads_summed"], 1)
            for n in range(1, 4):
                product(unit("prnn", n), rhs=yrT)
            for n in range(4):
                product(unit("patt", n), rhs=yaT, ready=None if n else lambda k: (s["att_ready"], k // 2 + 1))
            def logits(t):
                eng.wait_ge(s["ffn_low_out"], t + 1)
                eng.wait_ge(s["ffn_high_out"], t + 1)
                for k in range(KC):
                    ins = eng.matmul(bank[6 + t][0:NE, 0:P], wr[:, k, :], hfT[:, k, t * P:(t + 1) * P],
                                     start=(k == 0), stop=(k == KC - 1))
                ins.then_inc(s["logits_turned"], 1)

            def turn_logits(t):
                eng.wait_ge(s["logits_biased"], t + 1)
                eng.transpose(bank[2 + t][:, 0:NE], r_logT[:, t * P:(t + 1) * P], ident[0:NE, 0:NE]
                              ).then_inc(s["logits_done"], 1)

            for n in range(3):
                product(unit("out", n), lhsT=iT, ready=None if n else lambda k: (s["merged"], k // 2 + 1))
            turn(h2, 0, (s["ffn_low"], s["ffn_high"]), s["ffn_turned"])
            product(unit("out", 3), lhsT=iT)

            eng.wait_ge(s["router_loaded"], 32)
            logits(0)
            turn_logits(0)
            turn(h2, 1, (s["ffn_low"], s["ffn_high"]), s["ffn_turned"])
            logits(1)
            turn_logits(1)
            def keep_warm(n):
                for _ in range(n):
                    eng.matmul(bank[7][:, 0:T], ones[:, 0:P], ones[:, :], start=True, stop=True)

            keep_warm(2)
            eng.wait_ge(s["mixed"], 4)
            for ready, src, ps, turned in (("mask_ready", r_mask, bank[0], "mask_turned"),
                                           ("weight_ready", r_gate, bank[1], "weight_turned")):
                for t in range(TT):
                    eng.wait_ge(s[ready], t + 1)
                    ins = eng.transpose(ps[0:NE, t * P:(t + 1) * P], src[:, t, :], ident[:, :])
                ins.then_inc(s[turned], 1)
            keep_warm(1)
            eng.wait_ge(s["slots_ready"], 1)
            for t in range(TT):
                ins = eng.transpose(bank[0][:, t * NE:(t + 1) * NE], slotT[:, t * P:(t + 1) * P], ident[0:NE, 0:NE])
            ins.then_inc(s["slot_columns_done"], 1)
            keep_warm(1)

            def open_sum(n):
                t, h = divmod(n, 2)
                eng.matmul(bank[4 + n][:, :], gateT[:, t * P:(t + 1) * P], bdrow[:, h * CH:(h + 1) * CH],
                           start=True, stop=True, skip_group_check=True)

            eng.wait_ge(s["overflow_ready"], 1)
            eng.wait_ge(s["constants_ready"], 7)
            eng.matmul(bank[3][0:NE, 0:1], tri[:, :], novf, start=True, stop=True)
            eng.matmul(bank[3][0:1, 1:2], ones[0:NE, 0:1], novf, start=True, stop=True).then_inc(s["ends_done"], 1)

            def pair(ps, lhsT, w, swap=0, **flags):
                for h in range(2):
                    b = h ^ swap
                    ins = eng.matmul(ps[b * JB:(b + 1) * JB, :], lhsT, w[:, h * CH:(h + 1) * CH], **flags)
                return ins

            def block_of(turned, k):
                return turned[:, k % 4, (k // 4) * JB:(k // 4 + 1) * JB]

            def gather():
                for t in range(TT):
                    ins = pair(bank[2], sel[:, t, :], h2[:, t, :], start=(t == 0), stop=(t == TT - 1))
                ins.then_inc(job["gathered"], 1)

            def turn_gather():
                for c in range(4):
                    ins = eng.transpose(bank[2][:, c * P:(c + 1) * P], xg[:, c * P:(c + 1) * P], ident[:, :])
                ins.then_inc(job["gather_turned"], 1)

            eng.sem_inc(job["scattered_first"], 1)
            eng.sem_inc(job["scattered"], 1)
            eng.sem_inc(job["scatter_turned"], 1)
            eng.sem_inc(job["activation_turned"], 1)
            keep_warm(1)
            eng.wait_ge(job["selection"], 1)
            gather()
            eng.wait_ge(s["jobs_ready"], 1)
            eng.wait_ge(s["weight_out"], 1)
            for t in range(TT):
                o = t * MORE
                eng.matmul(bank[3][:, o:o + MORE], slotT[:, t * P:(t + 1) * P], ohj[0:NE, NE:JOBS],
                           start=True, stop=False)
                eng.matmul(bank[3][:, o:o + MORE], ones[0:NE, 0:P], block64, start=False, stop=True)
            for t in range(TT):
                o = TT * MORE + t * JOBS
                eng.matmul(bank[3][:, o:o + JOBS], gateT[0:NE, t * P:(t + 1) * P], ohj[0:NE, :], start=True, stop=True)
            eng.matmul(bank[3][0:1, 256:256 + JOBS], ecol[:, :], ohj[0:NE, :], start=True, stop=True
                       ).then_inc(s["late_columns_done"], 1)
            eng.wait_ge(job["gather_out"], 1)
            turn_gather()

            def contraction(m, parity, ps, row, w, arrived, count, ready, between=None, n=None):
                for q in range(NQ):
                    if q == NQ - 1 and between is not None:
                        between()
                    eng.wait_ge(arrived[q], count)
                    for k in (2 * q, 2 * q + 1):
                        ins = pair(ps, block_of(xgT[parity], k), w[:, k, :], start=(k == 0), stop=False)
                    ins.then_inc(used[m], 1)
                if n is not None:
                    eng.wait_ge(job["expert_onehot"], n)
                pair(ps, ohb, brow[:, row, :], start=False, stop=True).then_inc(job[ready], 1)

            def gate(n, parity, count, between=None):
                eng.wait_ge(job["input"], n)
                place = ("gate", "gate_odd")[parity]
                contraction("gate", parity, bank[0], 0, (WG, WG_ODD)[parity], loaded[place], count, "gate_done", between,
                            n)

            def one_job(j, parity, next_count=None):
                def turn_next():
                    eng.wait_ge(job["gather_out"], j + 2)
                    turn_gather()

                def turn_activation():
                    eng.wait_ge(job["activation"], j + 2)
                    for c in range(4):
                        ins = eng.transpose(bank[1][:, c * P:(c + 1) * P], av[:, c * P:(c + 1) * P], ident[:, :])
                    ins.then_inc(job["activation_turned"], 1)

                eng.wait_ge(job["activation_out"], j + 1)
                contraction("up", parity, bank[1], 1, WU, loaded["up"], j * 16 + 16, "up_done", turn_next)
                eng.wait_ge(job["weighted_selection"], j + 1)
                eng.wait_ge(job["output_out"], j + 1)
                for t in range(TT):
                    ins = eng.transpose(bank[3][:, t * P:(t + 1) * P], selw[:, t, :], ident[:, :])
                ins.then_inc(job["scatter_turned"], 1)
                if next_count is not None:
                    eng.wait_ge(job["gate_clamped"], j + 1)
                    gate(j + 2, 1 - parity, next_count, turn_activation)
                else:
                    turn_activation()
                eng.wait_ge(job["activation_out"], j + 2)
                for q in range(NQ):
                    eng.wait_ge(loaded["down"][q], j * 16 + 16)
                    for k in (2 * q, 2 * q + 1):
                        ins = pair(bank[3], block_of(avT, k), WD[:, k, :], swap=parity, start=(k == 0), stop=(k == KC - 1))
                    ins.then_inc(used["down"] if q < NQ - 1 else job["down_done"], 1)
                if next_count is not None:
                    eng.wait_ge(job["input"], j + 2)
                    eng.wait_ge(job["selection"], j + 3)
                    gather()
                if parity == 1:
                    eng.wait_ge(job["scatter_ready"], j + 1)
                    eng.wait_ge(job["output_half_out"], j + 1)
                    for t in range(TT):
                        for h in range(2):
                            if (t, h) == (0, 1):
                                eng.wait_ge(job["output_out"], j + 2)
                            ins = eng.matmul(bank[4 + 2 * t + h][:, :], scat[:, h, t, :], ys[h], start=False,
                                             stop=True, skip_group_check=True)
                            ins.then_inc(job["scattered_first"] if t == 0 else job["scattered"], 1)

            eng.wait_ge(s["bias_rows_loaded"], 48)
            open_sum(0)
            open_sum(1)
            gate(1, 0, 16)
            for n in range(2, 4):
                open_sum(n)
            eng.wait_ge(job["selection"], 2)
            gather()
            eng.wait_ge(s["job_table_ready"], 1)
            last_pair = eng.value_load(jobi[0:1, JOBS + 1:JOBS + 2], min_val=NE - 2, max_val=JOBS - 4)
            with eng.Fori(0, last_pair, 2) as j:
                one_job(j, 0, j * 8 + 16)
                one_job(j + 1, 1, j * 8 + 32)
            one_job(last_pair, 0, last_pair * 8 + 16)
            one_job(last_pair + 1, 1)


_INS = ["x", "norm_mix_g", "w_in", "conv_w", "conv_b", "w_rg_a", "b_rg_a", "w_rg_x", "b_rg_x", "lru_lambda",
        "diff_lambda_q1", "diff_lambda_k1", "diff_lambda_q2", "diff_lambda_k2", "subln_g", "rel_bias_table",
        "w_proj_rnn", "w_proj_att", "w_out", "norm_ffn_g", "w_router", "b_router", "w_gate_e", "b_gate_e",
        "w_up_e", "b_up_e", "w_down_e", "b_down_e", "norm_final_g"]


def kernel(**inputs):
    from concourse import bacc
    from concourse.bass_utils import run_bass_kernel_spmd

    nc = bacc.Bacc("TRN2", target_bir_lowering=False, num_devices=1)
    arrays, args = {}, {}
    for name in _INS:
        a = np.ascontiguousarray(inputs[name])
        arrays[f"in_{name}"] = a
        args[name] = nc.dram_tensor(f"in_{name}", a.shape, mybir.dt.from_np(a.dtype), kind="ExternalInput").ap()
    arrays["in_bucket_onehot"] = bucket_onehot()
    args["bucket_onehot"] = nc.dram_tensor("in_bucket_onehot", (NBUCKET + 1, DIFFS), F32, kind="ExternalInput").ap()
    result = nc.dram_tensor("out_0", (1, T, D), F32, kind="ExternalOutput").ap()
    hybrid_block(nc, args, result)
    r = run_bass_kernel_spmd(nc, [arrays], core_ids=[0])
    return r.results[0]["out_0"]
```
